# Optimizing a Trainium2 kernel written in Bass

```python
import jax, jax.numpy as jnp
from jax import lax
import numpy as np

D_MODEL = 1024
BATCH = 1
SEQ = 512
DEPTH = 2
DEC_BATCH = 1
DEC_SEQ = 64
PAST_LEN = 256

CHUNK = 64
N_MIXERS = 2
N_LAYERS_A = (DEPTH + 1) // 2
N_LAYERS_B = DEPTH // 2
HEAD_DIM = 64
N_HEADS_A = 16
N_KV_A = 4
GQA_REP = N_HEADS_A // N_KV_A
N_IDX_HEADS = 8
IDX_DIM = 64
IDX_ROPE_DIM = 32
TOPK_CAP = 256
N_HEADS_B = 16
D_FF = -(-8 * D_MODEL // (3 * 256)) * 256
ROPE_THETA = 10000.0
QBLOCK = 128
EPS = 1e-6
FORGET_BIAS_MEAN = 3.0
A_WIDTHS = (N_HEADS_A * HEAD_DIM, N_KV_A * HEAD_DIM, N_KV_A * HEAD_DIM, N_IDX_HEADS * IDX_DIM, IDX_DIM, N_IDX_HEADS)
A_IN = sum(A_WIDTHS)
B_INNER = N_HEADS_B * HEAD_DIM
B_WIDTHS = (B_INNER, B_INNER, B_INNER, B_INNER, N_HEADS_B)
B_IN = sum(B_WIDTHS)

kernel_name = "dsa_fox_streaming_encoder_step"

def split_cols(x, widths):
    outs, off = [], 0
    for w in widths:
        outs.append(x[..., off:off + w])
        off += w
    return outs

def rms_norm(x, g):
    xf = x.astype(jnp.float32)
    y = xf * lax.rsqrt(jnp.mean(xf * xf, axis=-1, keepdims=True) + EPS)
    return (y * g.astype(jnp.float32)).astype(x.dtype)

def ada_modulate(h, shift, scale):
    return h * (1.0 + scale[:, None, :]) + shift[:, None, :]

def rope(x, pos):
    half = x.shape[-1] // 2
    inv = ROPE_THETA ** (-jnp.arange(half, dtype=jnp.float32) / half)
    ang = pos.astype(jnp.float32)[:, None] * inv[None, :]
    cos = jnp.cos(ang)[:, None, :]
    sin = jnp.sin(ang)[:, None, :]
    xf = x.astype(jnp.float32)
    x1, x2 = xf[..., :half], xf[..., half:]
    return jnp.concatenate([x1 * cos - x2 * sin, x2 * cos + x1 * sin], axis=-1).astype(x.dtype)

def partial_rope(x, pos):
    return jnp.concatenate([rope(x[..., :IDX_ROPE_DIM], pos), x[..., IDX_ROPE_DIM:]], axis=-1)

def sweep_queries(fn, q_pos, *qs):
    tq = q_pos.shape[0]
    qb = min(QBLOCK, tq)
    nb = tq // qb

    def split(a):
        return jnp.moveaxis(a.reshape(a.shape[0], nb, qb, *a.shape[2:]), 1, 0)

    out = lax.map(lambda blk: fn(*blk), (q_pos.reshape(nb, qb), *[split(a) for a in qs]))
    out = jnp.moveaxis(out, 0, 1)
    return out.reshape(out.shape[0], tq, *out.shape[3:])

def dsa_mixer(h, pos, w_in, w_out, past):
    b, t, _ = h.shape
    q, k, v, qi, ki, wi = split_cols(h @ w_in, A_WIDTHS)
    q = rope(q.reshape(b, t, N_HEADS_A, HEAD_DIM), pos)
    k = rope(k.reshape(b, t, N_KV_A, HEAD_DIM), pos)
    v = v.reshape(b, t, N_KV_A, HEAD_DIM)
    qi = partial_rope(qi.reshape(b, t, N_IDX_HEADS, IDX_DIM), pos)
    ki = partial_rope(ki.reshape(b, t, 1, IDX_DIM), pos)[:, :, 0]
    wi = wi * (N_IDX_HEADS ** -0.5 * IDX_DIM ** -0.5)
    if past is None:
        k_all, v_all, ki_all = k, v, ki
    else:
        pk, pv, pki = past
        k_all = jnp.concatenate([pk.astype(k.dtype), k], axis=1)
        v_all = jnp.concatenate([pv.astype(v.dtype), v], axis=1)
        ki_all = jnp.concatenate([pki.astype(ki.dtype), ki], axis=1)
    n_keys = k_all.shape[1]
    topk = min(TOPK_CAP, n_keys // 4)
    key_chunk = jnp.arange(n_keys, dtype=jnp.int32) // CHUNK

    def block(qp, qb, qib, wib):
        nq = qp.shape[0]
        rel = jax.nn.relu(jnp.einsum('bqhd,bsd->bqhs', qib, ki_all).astype(jnp.float32))
        score = jnp.einsum('bqhs,bqh->bqs', rel, wib.astype(jnp.float32))
        q_chunk = qp // CHUNK
        adm = key_chunk[None, :] <= q_chunk[:, None]
        score = jnp.where(adm[None], score, -jnp.inf)
        _, idx = lax.top_k(score, topk)
        k_sel = jax.vmap(lambda kb, ib: kb[ib])(k_all, idx)
        v_sel = jax.vmap(lambda vb, ib: vb[ib])(v_all, idx)
        valid = key_chunk[idx] <= q_chunk[None, :, None]
        qg = qb.reshape(b, nq, N_KV_A, GQA_REP, HEAD_DIM)
        logit = jnp.einsum('bqgrd,bqkgd->bqgrk', qg, k_sel).astype(jnp.float32) * (HEAD_DIM ** -0.5)
        logit = jnp.where(valid[:, :, None, None, :], logit, -jnp.inf)
        p = jax.nn.softmax(logit, axis=-1).astype(v_sel.dtype)
        o = jnp.einsum('bqgrk,bqkgd->bqgrd', p, v_sel)
        return o.reshape(b, nq, N_HEADS_A * HEAD_DIM)

    o = sweep_queries(block, pos, q, qi, wi)
    return o @ w_out, (k, v, ki)

def fox_mixer(h, pos, w_in, b_forget, w_out, past):
    b, t, _ = h.shape
    q, k, v, g, f = split_cols(h @ w_in, B_WIDTHS)
    q = q.reshape(b, t, N_HEADS_B, HEAD_DIM)
    k = k.reshape(b, t, N_HEADS_B, HEAD_DIM)
    v = v.reshape(b, t, N_HEADS_B, HEAD_DIM)
    logf = jax.nn.log_sigmoid(f.astype(jnp.float32) + b_forget.astype(jnp.float32))
    if past is None:
        k_all, v_all, lf_all = k, v, logf
    else:
        pk, pv, plf = past
        k_all = jnp.concatenate([pk.astype(k.dtype), k], axis=1)
        v_all = jnp.concatenate([pv.astype(v.dtype), v], axis=1)
        lf_all = jnp.concatenate([plf.astype(jnp.float32), logf], axis=1)
    n_keys = k_all.shape[1]
    cum = jnp.cumsum(lf_all, axis=1)
    cum_keys = jnp.transpose(cum, (0, 2, 1))
    cum_q = cum[:, n_keys - t:]
    key_pos = jnp.arange(n_keys, dtype=jnp.int32)

    def block(qp, qb, cqb):
        nq = qp.shape[0]
        logit = jnp.einsum('bqhd,bshd->bhqs', qb, k_all).astype(jnp.float32) * (HEAD_DIM ** -0.5)
        logit = logit + (jnp.transpose(cqb, (0, 2, 1))[:, :, :, None] - cum_keys[:, :, None, :])
        causal = key_pos[None, :] <= qp[:, None]
        logit = jnp.where(causal[None, None], logit, -jnp.inf)
        p = jax.nn.softmax(logit, axis=-1).astype(v_all.dtype)
        o = jnp.einsum('bhqs,bshd->bqhd', p, v_all)
        return o.reshape(b, nq, B_INNER)

    o = sweep_queries(block, pos, q, cum_q)
    o = o * jax.nn.sigmoid(g)
    return o @ w_out, (k, v, logf)

def swiglu(h, w_in, w_out):
    gate, up = split_cols(h @ w_in, (D_FF, D_FF))
    return (jax.nn.silu(gate) * up) @ w_out

def run_trunk(x, c, pos, caches, w_ada, b_ada, g_mix, g_ffn, w_in_a, w_out_a, w_in_b, b_forget, w_out_b,
              w_ffn_in, w_ffn_out, w_ada_final, b_ada_final, g_final):
    a_k, a_v, a_ki, b_k, b_v, b_lf = [], [], [], [], [], []
    cs = jax.nn.silu(c)
    for i in range(DEPTH):
        sh1, sc1, gt1, sh2, sc2, gt2 = jnp.split(cs @ w_ada[i] + b_ada[i], 6, axis=-1)
        h = ada_modulate(rms_norm(x, g_mix[i]), sh1, sc1)
        j = i // N_MIXERS
        if i % N_MIXERS == 0:
            past = None if caches is None else (caches[0][j], caches[1][j], caches[2][j])
            o, (k, v, ki) = dsa_mixer(h, pos, w_in_a[j], w_out_a[j], past)
            a_k.append(k); a_v.append(v); a_ki.append(ki)
        else:
            past = None if caches is None else (caches[3][j], caches[4][j], caches[5][j])
            o, (k, v, lf) = fox_mixer(h, pos, w_in_b[j], b_forget[j], w_out_b[j], past)
            b_k.append(k); b_v.append(v); b_lf.append(lf)
        x = x + gt1[:, None, :] * o
        h = ada_modulate(rms_norm(x, g_ffn[i]), sh2, sc2)
        x = x + gt2[:, None, :] * swiglu(h, w_ffn_in[i], w_ffn_out[i])
    shf, scf = jnp.split(cs @ w_ada_final + b_ada_final, 2, axis=-1)
    y = ada_modulate(rms_norm(x, g_final), shf, scf)
    return y, (jnp.stack(a_k), jnp.stack(a_v), jnp.stack(a_ki), jnp.stack(b_k), jnp.stack(b_v), jnp.stack(b_lf))

def setup_inputs(seed: int = 0) -> dict:
    key = jax.random.key(seed)
    ks = jax.random.split(key, 24)

    def nrm(k, shape, s):
        return jax.random.normal(k, shape, jnp.float32) * s

    d = D_MODEL
    return {
        "x_prompt": nrm(ks[0], (BATCH, SEQ, d), 1.0),
        "x_sample": nrm(ks[1], (DEC_BATCH, DEC_SEQ, d), 1.0),
        "cache_a_k": nrm(ks[2], (N_LAYERS_A, DEC_BATCH, PAST_LEN, N_KV_A, HEAD_DIM), 1.0),
        "cache_a_v": nrm(ks[3], (N_LAYERS_A, DEC_BATCH, PAST_LEN, N_KV_A, HEAD_DIM), 1.0),
        "cache_a_kidx": nrm(ks[4], (N_LAYERS_A, DEC_BATCH, PAST_LEN, IDX_DIM), 1.0),
        "cache_b_k": nrm(ks[5], (N_LAYERS_B, DEC_BATCH, PAST_LEN, N_HEADS_B, HEAD_DIM), 1.0),
        "cache_b_v": nrm(ks[6], (N_LAYERS_B, DEC_BATCH, PAST_LEN, N_HEADS_B, HEAD_DIM), 1.0),
        "cache_b_logf": jax.nn.log_sigmoid(FORGET_BIAS_MEAN + nrm(ks[7], (N_LAYERS_B, DEC_BATCH, PAST_LEN, N_HEADS_B), 1.0)),
        "c_prompt": nrm(ks[8], (BATCH, d), 1.0),
        "c_sample": nrm(ks[9], (DEC_BATCH, d), 1.0),
        "w_ada": nrm(ks[10], (DEPTH, d, 6 * d), 0.5 * d ** -0.5),
        "b_ada": nrm(ks[11], (DEPTH, 6 * d), 0.01),
        "g_mix": 1.0 + nrm(ks[12], (DEPTH, d), 0.02),
        "g_ffn": 1.0 + nrm(ks[13], (DEPTH, d), 0.02),
        "w_in_a": nrm(ks[14], (N_LAYERS_A, d, A_IN), d ** -0.5),
        "w_out_a": nrm(ks[15], (N_LAYERS_A, N_HEADS_A * HEAD_DIM, d), (N_HEADS_A * HEAD_DIM) ** -0.5),
        "w_in_b": nrm(ks[16], (N_LAYERS_B, d, B_IN), d ** -0.5),
        "b_forget": FORGET_BIAS_MEAN + nrm(ks[17], (N_LAYERS_B, N_HEADS_B), 0.1),
        "w_out_b": nrm(ks[18], (N_LAYERS_B, B_INNER, d), B_INNER ** -0.5),
        "w_ffn_in": nrm(ks[19], (DEPTH, d, 2 * D_FF), d ** -0.5),
        "w_ffn_out": nrm(ks[20], (DEPTH, D_FF, d), D_FF ** -0.5),
        "w_ada_final": nrm(ks[21], (d, 2 * d), 0.5 * d ** -0.5),
        "b_ada_final": nrm(ks[22], (2 * d,), 0.01),
        "g_final": 1.0 + nrm(ks[23], (d,), 0.02),
    }

def reference(x_prompt, x_sample, cache_a_k, cache_a_v, cache_a_kidx, cache_b_k, cache_b_v, cache_b_logf,
              c_prompt, c_sample, w_ada, b_ada, g_mix, g_ffn, w_in_a, w_out_a, w_in_b, b_forget, w_out_b,
              w_ffn_in, w_ffn_out, w_ada_final, b_ada_final, g_final):
    pos_p = jnp.arange(x_prompt.shape[1], dtype=jnp.int32)
    pos_s = cache_a_k.shape[2] + jnp.arange(x_sample.shape[1], dtype=jnp.int32)
    y_prompt, (pak, pav, paki, pbk, pbv, pblf) = run_trunk(
        x_prompt, c_prompt, pos_p, None, w_ada, b_ada, g_mix, g_ffn, w_in_a, w_out_a, w_in_b, b_forget,
        w_out_b, w_ffn_in, w_ffn_out, w_ada_final, b_ada_final, g_final)
    y_sample, (sak, sav, saki, sbk, sbv, sblf) = run_trunk(
        x_sample, c_sample, pos_s, (cache_a_k, cache_a_v, cache_a_kidx, cache_b_k, cache_b_v, cache_b_logf),
        w_ada, b_ada, g_mix, g_ffn, w_in_a, w_out_a, w_in_b, b_forget, w_out_b, w_ffn_in, w_ffn_out,
        w_ada_final, b_ada_final, g_final)
    return (y_prompt, y_sample, pak, pav, paki, pbk, pbv, pblf, sak, sav, saki, sbk, sbv, sblf)


_drawn_inputs = setup_inputs


def setup_inputs(seed=0):
    import zlib

    import numpy as np

    out = dict(_drawn_inputs(seed))
    spreads = {}
    factors = {'cache_b_k': 4.822,
     'cache_b_v': 3.725,
     'cache_b_logf': 8.0,
     'b_ada': 3.345,
     'g_mix': 2.806,
     'g_ffn': 7.159,
     'b_ada_final': 4.275,
     'g_final': 3.028}
    for name, (base, spread) in spreads.items():
        noise = np.random.default_rng([zlib.crc32(name.encode()), seed]).standard_normal(out[name].shape)
        drawn = base * np.exp(spread * noise) if base else spread * noise
        out[name] = __import__('jax').numpy.asarray(drawn.astype(out[name].dtype))
    for name, factor in factors.items():
        out[name] = (out[name] * factor).astype(out[name].dtype)
    return out
```

```python
from contextlib import ExitStack

import numpy as np
import concourse.bass as bass
from concourse import mybir
from concourse.alu_op_type import AluOpType as ALU

F32 = mybir.dt.float32
F32R = mybir.dt.float32r
BF16 = mybir.dt.bfloat16
ACT = mybir.ActivationFunctionType
ds = bass.ds

P = 128
D = 1024
NP_, NS = 512, 64
TOK = NP_ + NS
HALF = TOK // 2
PAST = 256
NK = NP_ + PAST + NS
HD = 64
KT = D // P
NQT = NP_ // P
PAIRS = 8
NG = 4
DFF = 2816
HT = DFF // P // 2
NIDX = 8
TOPK_P, TOPK_S = 128, 80
THETA, EPS = 10000.0, 1e-6
NEG = -1e30
FILL, TAKEN = -3.0e38, -3.4e38
WCOL = HT * P
QSCALE = HD ** -0.5
OFF = [0, 128, 384, 768]
SOFF = 1280

U_KIW = 0
U_QI = 1
U_K = 5
U_V = 7
U_Q = 9
U_OA = U_Q + PAIRS
U_F0 = U_OA + KT
FFN_N = 2 * HT + KT
U_FG = U_F0 + 2 * FFN_N
U_B = U_FG + 1
U_OB = U_B + 4 * PAIRS
U_F1 = U_OB + KT

T_ROWS, T_X, T_KC, T_KIC, T_ADA0 = 0, 2, 12, 14, 15
T_KIW = 16
T_K0, T_V0 = 17, 21
T_ADA1 = 25
T_ADA2 = 26
T_A = 27
T_ADA3 = T_A + 9 * PAIRS
T_LF = T_ADA3 + 4
T_B0 = T_LF + 2
T_B = T_B0 + 4
T_Y = T_B + 13 * (PAIRS - 1) + 9

ACT_N0, ACT_OA, ACT_N1, ACT_N2, ACT_OB, ACT_N3 = (KT * i for i in range(6))


def rope_of(u):
    return u if u < U_V else u - 2


def host_constants():
    pos = np.concatenate([np.arange(NP_), PAST + np.arange(NS)]).astype(np.float32)
    ident = np.eye(P, dtype=np.float32)
    tri = np.where(np.arange(P)[None, :] <= np.arange(P)[:, None], 0.0, NEG).astype(np.float32)
    out = [ident, tri]
    tables = []
    for half in (32, 16):
        perm = np.zeros((P, P), np.float32)
        cos = np.ones((P, TOK), np.float32)
        sin = np.zeros((P, TOK), np.float32)
        inv = (np.float32(THETA) ** (-np.arange(half, dtype=np.float32) / np.float32(half))).astype(np.float32)
        ang = (pos[:, None] * inv[None, :]).astype(np.float32)
        for h in range(2):
            for d in range(2 * half):
                row = 64 * h + d
                first = d < half
                perm[row + half if first else row - half, row] = 1.0
                cos[row] = np.cos(ang[:, d % half])
                sin[row] = np.sin(ang[:, d % half]) * (-1.0 if first else 1.0)
        out.append(perm)
        tables += [cos, sin]
    return np.concatenate(out + tables, axis=1).astype(np.float32)


NCONST = 4 * P


def encoder_step(nc, i, o):
    ctx = ExitStack()
    with ctx:
        def sem(name):
            return ctx.enter_context(nc.semaphore(name))

        def sb(name, shape, dt=F32, scope=ctx):
            return scope.enter_context(nc.sbuf_tensor(name, shape, dt))

        x = sb("x", [P, KT, TOK])
        act_hi = sb("act_hi", [P, KT, TOK], F32R)
        act_lo = sb("act_lo", [P, KT, TOK], F32R)
        w_raw = sb("w_raw", [P, 2, WCOL])
        w_hi = sb("w_hi", [P, 2, WCOL], F32R)
        w_lo = sb("w_lo", [P, 2, WCOL], F32R)
        ada_raw = sb("ada_raw", [P, 2, 2048])
        consts = sb("consts", [P, NCONST])
        ident, tri = consts[:, 0:P], consts[:, P:2 * P]
        perm_q, perm_i = consts[:, 2 * P:3 * P], consts[:, 3 * P:4 * P]
        ident_b = sb("ident_b", [P, P], BF16)
        tri_b = sb("tri_b", [P, P], BF16)
        ones = sb("ones", [P, P])
        vecs = sb("vecs", [P, P])
        gains = sb("gains", [P, 40])
        cs_w = sb("cs_w", [P, KT, 32])
        ada_row = sb("ada_row", [P, 512])
        mods = sb("mods", [P, 112, 2])
        mulA = sb("mulA", [P, 5, KT, 2])
        bias_f = sb("bias_f", [16, 1])
        negmax = sb("negmax", [P, 2, 3])
        rowsum = sb("rowsum", [P, 2, 3])
        rinv = sb("rinv", [P, 2, 3])
        top8 = sb("top8", [P, 4, 8])
        eps = sb("eps", [P, 1])
        cell = sb("cell", [P, 1])

        s = ExitStack()
        rows1 = sb("rows1", [P, P], scope=s)
        rows2 = sb("rows2", [40, P], scope=s)
        x_in = sb("x_in", [P, 5, D], scope=s)
        s.close()
        s = ExitStack()
        fo = sb("fo", [P, KT, TOK], scope=s)
        y_tok = sb("y_tok", [P, 2, 512], scope=s)
        sb("norm_pad", [P, 2 * HT * TOK + 2 * TOK - KT * TOK - 2 * 512], scope=s)
        sq = sb("sq", [P, 2, TOK], scope=s)
        root = sb("root", [P, TOK], scope=s)
        rstd = sb("rstd", [P, TOK], scope=s)
        yb = sb("yb", [P, 2, TOK], scope=s)
        fb = sb("fb", [P, 2, TOK], scope=s)
        s.close()
        s = ExitStack()
        hid_hi = sb("hid_hi", [P, HT, TOK], F32R, scope=s)
        hid_lo = sb("hid_lo", [P, HT, TOK], F32R, scope=s)
        sg = sb("sg", [P, TOK], scope=s)
        hf = sb("hf", [P, TOK], scope=s)
        s.close()
        qo = sb("qo", [P, PAIRS, TOK])
        a = ExitStack()
        kT4 = sb("kT4", [P, NG, NK], scope=a)
        kiT = sb("kiT", [P, NK], scope=a)
        v4 = sb("v4", [P, 7, NG * HD], scope=a)
        sc = sb("sc", [P, SOFF + PAST + NS], scope=a)
        b = ExitStack()
        kout = sb("kout", [P, 5, NG * HD], scope=b)
        kiout = sb("kiout", [P, 5, HD], scope=b)
        b.close()
        b = ExitStack()
        kc_in = sb("kc_in", [P, 2, NG, 2, HD], scope=b)
        kic_in = sb("kic_in", [P, 2, 2, HD], scope=b)
        b.close()
        sb("kout_pad", [P, 5 * NG * HD + 5 * HD], scope=a)
        b = ExitStack()
        tables = sb("tables", [P, 4, TOK], scope=b)
        rawb = sb("rawb", [P, 2, TOK], scope=b)
        permb = sb("permb", [P, 2, TOK], scope=b)
        vTb = sb("vTb", [P, TOK], scope=b)
        kR = sb("kR", [P, TOK], scope=b)
        qiT = sb("qiT", [P, 4, TOK], scope=b)
        rel = sb("rel", [P, 2, 512], scope=b)
        wi_t = sb("wi_t", [P, 5, NIDX], scope=b)
        b.close()
        b = ExitStack()
        qS_a = sb("qS_a", [P, 2, TOK], scope=b)
        kS_a = sb("kS_a", [P, NK], scope=b)
        vS_a = sb("vS_a", [P, 7, HD], scope=b)
        pr_a = sb("pr_a", [P, 2, 2, 512], scope=b)
        ps_a = sb("ps_a", [P, PAST + NS], scope=b)
        pT_a = sb("pT_a", [P, 2, 512], scope=b)
        pTs_a = sb("pTs_a", [P, 3, P], scope=b)
        b.close()
        a.close()
        b = ExitStack()
        fw = ExitStack()
        zb = sb("zb", [16, TOK], scope=fw)
        eb = sb("eb", [16, TOK], scope=fw)
        ub = sb("ub", [16, TOK], scope=fw)
        lb = sb("lb", [16, TOK], scope=fw)
        lfs = sb("lfs", [16, PAST + NS], scope=fw)
        cum = sb("cum", [16, NK], scope=fw)
        one_row = sb("one_row", [16, 512], scope=fw)
        lfc = sb("lfc", [P, 2, 16], scope=fw)
        lf_tok = sb("lf_tok", [P, 5, 16], scope=fw)
        fw.close()
        pr_b = sb("pr_b", [P, 2, 2, 512], scope=b)
        ps_b = sb("ps_b", [P, PAST + NS], scope=b)
        pT_b = sb("pT_b", [P, 2, 512], scope=b)
        pTs_b = sb("pTs_b", [P, 3, P], scope=b)
        sb("forget_pad", [P, 512], scope=b)
        qS_b = sb("qS_b", [P, 2, TOK], scope=b)
        kS_b = sb("kS_b", [P, 2, NK], scope=b)
        vS_b = sb("vS_b", [P, 2, 7, P], scope=b)
        vTb_b = sb("vTb_b", [P, TOK], scope=b)
        kout_b = sb("kout_b", [P, 5, P], scope=b)
        kc_b = sb("kc_b", [P, 2, 2, P], scope=b)
        bk = sb("bk", [P, 2, 2, NK], scope=b)
        gsig = sb("gsig", [P, 2, TOK], scope=b)
        b.close()

        lin = ctx.enter_context(nc.psum_tensor("lin", [P, 2, 2, 512], F32))
        S = ctx.enter_context(nc.psum_tensor("S", [P, 2, 512], F32))
        T = ctx.enter_context(nc.psum_tensor("T", [P, 512], F32))
        O = ctx.enter_context(nc.psum_tensor("O", [P, 512], F32))
        cum_dram = nc.dram_tensor("cum_dram", [16, NK], F32, kind="Internal").ap()

        const_in = sem("const_in")
        rows_in = sem("rows_in")
        x_loaded = [sem(f"x_loaded{t}") for t in range(5)]
        cache_in = sem("cache_in")
        raw_in = [sem("raw_in0"), sem("raw_in1")]
        whi_done, wlo_done = sem("whi_done"), sem("wlo_done")
        mm_done = sem("mm_done")
        lin_free = [sem("lin_free0"), sem("lin_free1")]
        ada_in = [sem("ada_in0"), sem("ada_in1")]
        ada_used, ada_row_done = sem("ada_used"), sem("ada_row_done")
        cs_zero, cs_done, ones_done = sem("cs_zero"), sem("cs_done"), sem("ones_done")
        t_ready, t_free = sem("t_ready"), sem("t_free")
        muls_step = sem("muls_step")
        sq_done, ss_done, root_done, rstd_done = sem("sq_done"), sem("ss_done"), sem("root_done"), sem("rstd_done")
        y_done, f_done, acthi_done, act_ready = sem("y_done"), sem("f_done"), sem("acthi_done"), sem("act_ready")
        raw_done, perm_done, rope_step, rope_done = sem("raw_done"), sem("perm_done"), sem("rope_step"), sem("rope_done")
        kdup_done, kidup_done = sem("kdup_done"), sem("kidup_done")
        idx_done, rel_done, sc_step = sem("idx_done"), sem("rel_done"), sem("sc_step")
        top_step, mask_done = sem("top_step"), sem("mask_done")
        out_sent, kv_sent = sem("out_sent"), sem("kv_sent")
        q_staged, k_staged, v_staged = sem("q_staged"), sem("k_staged"), sem("v_staged")
        s_done, max_done, exp_done, rinv_done, norm_done = (
            sem("s_done"), sem("max_done"), sem("exp_done"), sem("rinv_done"), sem("norm_done"))
        pv_done, o_free = sem("pv_done"), sem("o_free")
        hidhi_done, hid_ready, silu_done = sem("hidhi_done"), sem("hid_ready"), sem("silu_done")
        z_done, lf_act, lf_dve = sem("z_done"), sem("lf_act"), sem("lf_dve")
        cum_out = sem("cum_out")
        bk_in = [sem("bk_in0"), sem("bk_in1")]
        kvc_in = [sem("kvc_in0"), sem("kvc_in1")]
        lfc_in = sem("lfc_in")
        gsig_step = sem("gsig_step")
        y_sent = [sem("y_sent0"), sem("y_sent1")]

        block = ctx.enter_context(nc.Block())

        def free_count(u):
            return u // 2 + 1

        @block.sync
        def _(sp):
            sp.dma_start(consts[:, :], i["consts"][:, 0:NCONST]).then_inc(const_in, 16)
            sp.dma_start(rows1[0:96, :], i["b_ada"].rearrange("l (r p) -> (l r) p", p=P)).then_inc(rows_in, 16)
            sp.dma_start(rows1[96:112, :], i["b_ada_final"].rearrange("(r p) -> r p", p=P)).then_inc(rows_in, 16)
            sp.dma_start(rows1[112:120, :], i["c_prompt"].rearrange("b (r p) -> (b r) p", p=P)).then_inc(rows_in, 16)
            sp.dma_start(rows1[120:128, :], i["c_sample"].rearrange("b (r p) -> (b r) p", p=P)).then_inc(rows_in, 16)
            sp.dma_start(rows2[0:16, :], i["g_mix"].rearrange("l (r p) -> (l r) p", p=P)).then_inc(rows_in, 16)
            sp.dma_start(rows2[16:32, :], i["g_ffn"].rearrange("l (r p) -> (l r) p", p=P)).then_inc(rows_in, 16)
            sp.dma_start(rows2[32:40, :], i["g_final"].rearrange("(r p) -> r p", p=P)).then_inc(rows_in, 16)
            sp.dma_start(bias_f[:, :], i["b_forget"].rearrange("l n -> n l")).then_inc(rows_in, 16)

            def ada_load(n, src, par=None, half=None):
                par = n % 2 if par is None else par
                half = n // 2 if half is None else half
                if half > 0:
                    sp.wait_ge(ada_used, 2 * half + par - 1)
                sp.dma_start(ada_raw[:, par, :], src).then_inc(ada_in[par], 16)

            def ada_src(b, kt):
                rows = slice(kt * P, (kt + 1) * P)
                if b == 6:
                    return i["w_ada_final"][rows, :]
                return i["w_ada"][b // 3, rows, (b % 3) * 2048:(b % 3 + 1) * 2048]

            ada_load(0, ada_src(0, 0))
            ada_load(1, ada_src(0, 1))
            for t in range(4):
                sp.dma_start(x_in[:, t, :], i["x_prompt"][0, t * P:(t + 1) * P, :]).then_inc(x_loaded[t], 16)
            sp.dma_start(x_in[0:NS, 4, :], i["x_sample"][0, :, :]).then_inc(x_loaded[4], 16)
            for dup in range(2):
                sp.dma_start(kc_in[:, 0, :, dup, :], i["cache_a_k"][0, 0, 0:P]).then_inc(cache_in, 16)
                sp.dma_start(kc_in[:, 1, :, dup, :], i["cache_a_k"][0, 0, P:2 * P]).then_inc(cache_in, 16)
                sp.dma_start(kic_in[:, :, dup, :],
                             i["cache_a_kidx"][0, 0].rearrange("(t p) d -> p t d", p=P)).then_inc(cache_in, 16)
            for kt in range(2, KT):
                ada_load(kt, ada_src(0, kt))

            def w_load(u, src, kt, cols, it=0, per=0):
                if u >= 2:
                    sp.wait_ge(wlo_done, per * it + u - 1)
                sp.dma_start(w_raw[:, u % 2, 0:kt * cols].rearrange("p (t n) -> p t n", t=kt),
                             src.rearrange("(t p) n -> p t n", p=P)).then_inc(raw_in[u % 2], 16)

            wa = i["w_in_a"][0]
            w_load(U_KIW, wa[:, 2048:2120], KT, 72)
            for j in range(4):
                w_load(U_QI + j, wa[:, 1536 + j * P:1536 + (j + 1) * P], KT, P)
                if j == 0:
                    sp.wait_ge(t_free, T_KIC + 1)
                    sp.wait_ge(act_ready, ACT_N0 + KT)
                    sp.dma_start(tables[:, :, :], i["consts"][:, NCONST:].rearrange("p (k t) -> p k t", k=4))\
                      .then_inc(const_in, 16)
                    sp.dma_start(v4[:, 4:6, :], i["cache_a_v"][0, 0].rearrange("(t p) g d -> p t (g d)", p=P))\
                      .then_inc(cache_in, 16)
            for j in range(2):
                w_load(U_K + j, wa[:, 1024 + j * P:1024 + (j + 1) * P], KT, P)
            for j in range(2):
                w_load(U_V + j, wa[:, 1280 + j * P:1280 + (j + 1) * P], KT, P)
            w_load(U_Q, wa[:, 0:P], KT, P)
            n = KT
            for j in range(1, PAIRS):
                w_load(U_Q + j, wa[:, j * P:(j + 1) * P], KT, P)
                for _ in range(ADA_STEPS[j - 1]):
                    ada_load(n, ada_src(n // KT, n % KT))
                    n += 1

            def out_loads(u0, w, kt):
                with sp.Fori(0, KT // 2) as it:
                    for r in range(2):
                        w_load(u0 + r, w[:, ds((2 * it + r) * P, P)], kt, P, it, 2)

            def ffn_half_loads(layer, half, u0, ada_b):
                wi, wo = i["w_ffn_in"][layer], i["w_ffn_out"][layer]
                t0 = half * HT

                def tile(u, t, it, per):
                    w_load(u, wi[:, ds(t * P, P)], KT, P, it, per)
                    w_load(u + 1, wi[:, ds(t * P + DFF, P)], KT, P, it, per)

                done = 0
                if ada_b is not None:
                    for batch in range(2):
                        for r in range(4):
                            t = t0 + 4 * batch + r
                            for g in range(2):
                                w_load(u0 + 8 * batch + 2 * r + g, wi[:, t * P + g * DFF:t * P + g * DFF + P], KT, P)
                                ada_load(KT * (ada_b + batch) + 2 * r + g, ada_src(ada_b + batch, 2 * r + g))
                    done = 8
                with sp.Fori(0, HT - done) as it:
                    tile(u0 + 2 * done, it + (t0 + done), it, 2)
                out_loads(u0 + 2 * HT, wo[half * WCOL:(half + 1) * WCOL, :], HT)

            out_loads(U_OA, i["w_out_a"][0], KT)
            ffn_half_loads(0, 0, U_F0, 3)
            ffn_half_loads(0, 1, U_F0 + FFN_N, 5)

            wb = i["w_in_b"][0]
            w_load(U_FG, wb[:, 4096:4112], KT, 16)
            sp.wait_ge(f_done, 3 * KT)
            sp.wait_ge(act_ready, ACT_N2 + KT)
            sp.dma_start(lfc[:, :, :], i["cache_b_logf"][0, 0].rearrange("(t p) h -> p t h", p=P)).then_inc(lfc_in, 16)

            def kv_cache_load(par, pair, it=0, guard=True):
                if guard:
                    sp.wait_ge(pv_done, 8 * it + guard)
                cols = ds(pair * P, P)
                sp.dma_start(kc_b[:, par, :, :],
                             i["cache_b_k"][0, 0].rearrange("(t p) h d -> p t (h d)", p=P)[:, :, cols])\
                  .then_inc(kvc_in[par], 16)
                sp.dma_start(vS_b[:, par, 4:6, :],
                             i["cache_b_v"][0, 0].rearrange("(t p) h d -> p t (h d)", p=P)[:, :, cols])\
                  .then_inc(kvc_in[par], 16)

            def bias_load(par, pair, it=0, guard=True):
                if guard:
                    sp.wait_ge(max_done, 8 * it + guard)
                for e in range(2):
                    sp.dma_start(bk[:, par, e, :], cum_dram[ds(pair * 2 + e, 1), :].partition_broadcast(P))\
                      .then_inc(bk_in[par], 16)

            kv_cache_load(0, 0, guard=False)
            for c in range(4):
                w_load(U_B + c, wb[:, c * D:c * D + P], KT, P)
            sp.wait_ge(cum_out, 16)
            bias_load(0, 0, guard=False)
            bias_load(1, 1, guard=False)
            kv_cache_load(1, 1, guard=False)
            for c in range(4):
                w_load(U_B + 4 + c, wb[:, c * D + P:c * D + 2 * P], KT, P)
            with sp.Fori(0, PAIRS // 2 - 1) as it:
                for r in range(2):
                    pair = 2 * it + r + 2
                    bias_load(r, pair, it, 4 * (PAIRS + r) + 4)
                    kv_cache_load(r, pair, it, 4 * (PAIRS + r) + 4)
                    for c in range(4):
                        w_load(U_B + 8 + 4 * r + c, wb[:, ds(pair * P + c * D, P)], KT, P, it, 8)
            out_loads(U_OB, i["w_out_b"][0], KT)
            ffn_half_loads(1, 0, U_F1, None)
            ffn_half_loads(1, 1, U_F1 + FFN_N, None)

            sp.wait_ge(out_sent, 16 * N_OUT_A)
            sp.wait_ge(kv_sent, 16 * 4 * PAIRS)
            for r in range(2):
                sp.wait_ge(y_sent[r], 16 * 5)

        @block.tensor
        def _(pe):
            def lin_part(u, part, kt, m, hi, lo, it=0, per=0, ready=None):
                steps = [(0, t) for t in range(kt)] + [(1, t) for t in range(kt)]
                cut = (3 * kt) // 4
                if part is not None:
                    steps = steps[:cut] if part == 0 else steps[cut:]
                if steps[0] == (0, 0):
                    pe.wait_ge(whi_done, per * it + u + 1)
                    if u >= 2:
                        pe.wait_ge(lin_free[u % 2], (per // 2) * it + u // 2)
                for low, t in steps:
                    if (low, t) == (1, 0):
                        pe.wait_ge(wlo_done, per * it + u + 1)
                    if not low and ready is not None:
                        pe.wait_ge(ready[0], ready[1] + t + 1)
                    w = (w_lo if low else w_hi)[:, u % 2, t * m:(t + 1) * m]
                    for h in range(2):
                        tok = slice(h * HALF, (h + 1) * HALF)
                        out = lin[0:m, u % 2, h, 0:HALF]
                        last = nc.tensor.matmul(out, w, hi[:, t, tok], start=(not low and t == 0),
                                                stop=bool(low and t == kt - 1))
                        if not low:
                            nc.tensor.matmul(out, w, lo[:, t, tok], start=False, stop=False)
                if steps[-1] == (1, kt - 1):
                    last.then_inc(mm_done, 1)

            def linear(u, kt=KT, m=P, it=0, per=0, ready=None, hi=act_hi, lo=act_lo):
                lin_part(u, None, kt, m, hi, lo, it, per, ready)

            def t_use(n, it=0, per=0):
                if n >= 1:
                    pe.wait_ge(t_free, per * it + n)

            def ada_step(n, first=False):
                b, kt = n // KT, n % KT
                pe.wait_ge(ada_in[n % 2], 16 * (n // 2 + 1))
                if kt == 0 and b >= 1:
                    pe.wait_ge(ada_row_done, b)
                for j in range(4):
                    last = nc.tensor.matmul(O[32 * j:32 * j + 32, 0:512], cs_w[:, kt, :],
                                            ada_raw[:, n % 2, 512 * j:512 * j + 512],
                                            start=(kt == 0), stop=(kt == KT - 1))
                last.then_inc(ada_used, 1)

            def ada_transpose(b, t):
                pe.wait_ge(ada_row_done, b + 1)
                t_use(t)
                for c in range(4):
                    last = nc.tensor.transpose(T[:, c * P:(c + 1) * P], ada_row[:, c * P:(c + 1) * P], ident)
                last.then_inc(t_ready, 1)

            pe.wait_ge(const_in, 16)
            pe.wait_ge(rows_in, 16 * 8)
            nc.tensor.transpose(T[:, 0:P], rows1[:, :], ident).then_inc(t_ready, 1)
            t_use(1)
            nc.tensor.transpose(T[:, 0:40], rows2[:, :], ident[0:40, 0:40]).then_inc(t_ready, 1)
            for t in range(5):
                pe.wait_ge(x_loaded[t], 16)
                w = P if t < 4 else NS
                for h in range(2):
                    t_use(T_X + 2 * t + h)
                    for j in range(4):
                        c = (4 * h + j) * P
                        last = nc.tensor.transpose(T[:, j * P:j * P + w], x_in[0:w, t, c:c + P], ident[0:w, 0:w])
                    last.then_inc(t_ready, 1)
            pe.wait_ge(cache_in, 16 * 6)
            for h in range(2):
                t_use(T_KC + h)
                for g in range(2):
                    for t in range(2):
                        last = nc.tensor.transpose(T[:, (2 * g + t) * P:(2 * g + t + 1) * P],
                                                   kc_in[:, t, 2 * h + g, :, :], ident)
                last.then_inc(t_ready, 1)
            t_use(T_KIC)
            for t in range(2):
                last = nc.tensor.transpose(T[:, t * P:(t + 1) * P], kic_in[:, t, :, :], ident)
            last.then_inc(t_ready, 1)
            pe.wait_ge(cs_done, 1)
            for kt in range(KT):
                ada_step(kt)
            ada_transpose(0, T_ADA0)

            def norm_sums(nz):
                if nz == 0:
                    pe.wait_ge(ones_done, 1)
                for kt in range(KT):
                    pe.wait_ge(sq_done, KT * nz + kt + 1)
                    for h in range(2):
                        last = nc.tensor.matmul(S[:, h, 0:HALF], ones[:, :], sq[:, kt % 2, h * HALF:(h + 1) * HALF],
                                                start=(kt == 0), stop=(kt == KT - 1))
                    last.then_inc(ss_done, 1)

            norm_sums(0)

            def rope_perm(u):
                r = rope_of(u)
                pe.wait_ge(raw_done, r + 1)
                rows, pm = (64, perm_i[0:64, 0:64]) if u == U_KIW else (P, perm_i if u < U_K else perm_q)
                for h in range(2):
                    last = nc.tensor.matmul(lin[0:rows, u % 2, h, 0:HALF], pm,
                                            rawb[0:rows, r % 2, h * HALF:(h + 1) * HALF], start=True, stop=True)
                last.then_inc(perm_done, 1)

            def token_major(src, t0):
                for e in range(2):
                    t_use(t0 + e)
                    for t in (range(4) if e == 0 else (4,)):
                        w = P if t < 4 else NS
                        last = nc.tensor.transpose(T[0:w, (t % 4) * P:(t % 4 + 1) * P],
                                                   src[:, t * P:t * P + w], ident)
                    last.then_inc(t_ready, 1)

            linear(U_KIW, m=72, ready=(act_ready, ACT_N0))
            linear(U_QI)
            rope_perm(U_KIW)
            linear(U_QI + 1)
            rope_perm(U_QI)
            linear(U_QI + 2)
            rope_perm(U_QI + 1)
            pe.wait_ge(rope_done, 1)
            t_use(T_KIW)
            for t in range(5):
                w = P if t < 4 else NS
                kcol = t * P if t < 4 else NP_ + PAST
                nc.tensor.transpose(T[0:w, t * 72:t * 72 + 64], kiT[0:64, kcol:kcol + w], ident[0:64, 0:64])
                last = nc.tensor.transpose(T[0:w, t * 72 + 64:t * 72 + 72], vTb[64:72, t * P:t * P + w],
                                           ident[64:72, 64:72])
            last.then_inc(t_ready, 1)
            linear(U_QI + 3)
            rope_perm(U_QI + 2)
            linear(U_K)
            rope_perm(U_QI + 3)

            def idx_unit(n):
                qt, j = 3 - n // 4, n % 4
                if n == 0:
                    pe.wait_ge(rope_done, 5)
                    pe.wait_ge(kidup_done, 1)
                if n >= 1:
                    pe.wait_ge(rel_done, n)
                rows, tok, keys, nk = ((P, qt * P, 0, (qt + 1) * P) if qt else (NS, NP_, NP_, PAST + NS))
                for e in range(2):
                    r = slice(64 * e, 64 * e + 64)
                    last = nc.tensor.matmul(S[0:rows, e, 0:nk], qiT[r, j, tok:tok + rows], kiT[r, keys:keys + nk],
                                            start=True, stop=True)
                last.then_inc(idx_done, 1)

            for j, u in enumerate((U_K + 1, U_V, U_V + 1, U_Q)):
                for part in range(2):
                    idx_unit(4 * j + 2 * part)
                    lin_part(u, part, KT, P, act_hi, act_lo)
                    idx_unit(4 * j + 2 * part + 1)
                if j == 0:
                    rope_perm(U_K)
                if j == 1:
                    rope_perm(U_K + 1)
                    pe.wait_ge(rope_done, rope_of(U_K) + 1)
                    token_major(kR, T_K0)
                if j == 2:
                    pe.wait_ge(rope_done, rope_of(U_K + 1) + 1)
                    token_major(kR, T_K0 + 2)
                    pe.wait_ge(lin_free[U_V % 2], free_count(U_V))
                    token_major(vTb, T_V0)
                if j == 3:
                    pe.wait_ge(lin_free[(U_V + 1) % 2], free_count(U_V + 1))
                    token_major(vTb, T_V0 + 2)
            n = KT
            for j in range(1, PAIRS):
                linear(U_Q + j)
                rope_perm(U_Q + j - 1)
                for _ in range(ADA_STEPS[j - 1]):
                    ada_step(n)
                    n += 1
                    if n == 2 * KT:
                        ada_transpose(1, T_ADA1)
            rope_perm(U_Q + PAIRS - 1)
            ada_transpose(2, T_ADA2)

            def s_unit(k, par, n, it, per, qS, kS, ready, forget):
                for q, v in ready:
                    pe.wait_ge(q, v)
                if n >= 1:
                    pe.wait_ge(max_done, per * it + n)
                groups = [(0, P, k * P, 0, (k + 1) * P, 384 if k == 0 else 0)]
                if k == 0:
                    groups.append((1, NS, NP_, NP_, PAST + NS, 0))
                for sample, rows, tok, key, nk, col in groups:
                    for e in range(2):
                        r = slice(64 * e, 64 * e + 64)
                        out = S[64 * e:64 * e + 64] if sample else S[0:P]
                        last = nc.tensor.matmul(out[:, e, col:col + nk], qS[r, tok:tok + rows],
                                                kS[r, key:key + nk], start=True, stop=not forget)
                    if forget:
                        for e in range(2):
                            r = slice(64 * e, 64 * e + 64)
                            c = col + nk - rows
                            if sample:
                                last = nc.tensor.matmul(S[r, e, c:c + rows], ident_b[r, r], tri_b[r, r],
                                                        start=False, stop=True)
                            else:
                                last = nc.tensor.matmul(S[:, e, c:c + rows], ident_b[:, :], tri_b[:, :],
                                                        start=False, stop=True)
                last.then_inc(s_done, 1)

            def t_unit(k, use, par, n, t, it, per, tper, pr, ps):
                if use == 0:
                    pe.wait_ge(norm_done, per * it + n + 1)
                t_use(t, it, tper)
                if k == 0 and use == 0:
                    for e in range(2):
                        last = nc.tensor.transpose(T[:, e * P:(e + 1) * P], pr[:, 0, e, 0:P], ident)
                elif k == 0:
                    for b in range(3):
                        w = P if b < 2 else NS
                        last = nc.tensor.transpose(T[0:w, b * P:(b + 1) * P], ps[:, b * P:b * P + w], ident)
                else:
                    for b in range(k + 1):
                        last = nc.tensor.transpose(T[:, b * P:(b + 1) * P], pr[:, k % 2, use, b * P:(b + 1) * P], ident)
                last.then_inc(t_ready, 1)

            def pv_unit(k, n, pair, t, it, per, tper, pT, pTs, vS, split):
                pe.wait_ge(t_free, tper * it + t + 1)
                if k == 0 and pair >= 1:
                    pe.wait_ge(o_free, (per // 4) * it + pair)
                if k == 0:
                    for b in range(3):
                        w = P if b < 2 else NS
                        for e in range(2):
                            v = vS[0:w, 4 + b, 64 * e:64 * e + 64] if split else vS[0:w, 4 + b, :]
                            last = nc.tensor.matmul(T[64 * e:64 * e + 64, 0:NS], v, pTs[0:w, b, 64 * e:64 * e + 64],
                                                    start=(b == 0), stop=(b == 2))
                    last.then_inc(t_ready, 1)
                for b in range(k + 1):
                    for e in range(2):
                        v = vS[:, b, 64 * e:64 * e + 64] if split else vS[:, b, :]
                        last = nc.tensor.matmul(O[64 * e:64 * e + 64, k * P:(k + 1) * P], v,
                                                pT[:, e, b * P:(b + 1) * P], start=(b == 0), stop=(b == k))
                last.then_inc(pv_done, 1)

            def a_ready(pair, it, first):
                out = [(q_staged, 2 * it + pair + 1)]
                if first:
                    out.append((k_staged, it + pair // 2 + 1))
                return out

            def a_body(it, last_turn):
                for r in range(2):
                    for k in range(4):
                        n = 4 * r + k
                        t = T_A + 9 * r + (0 if k == 0 else 1 + 2 * k)
                        t_unit(k, 0, r, n, t, it, 8, 18, pr_a, ps_a)
                        if not (last_turn and n == 7):
                            k2, r2 = (k + 1) % 4, r + (k == 3)
                            s_unit(k2, r2 % 2, n + 1, it, 8, qS_a[:, r2 % 2, :], kS_a,
                                   a_ready(r2, it, r2 == 2) if k2 == 0 else [], False)
                        t_unit(k, 1, r, n, t + 1, it, 8, 18, pr_a, ps_a)
                        if n == 0:
                            pe.wait_ge(v_staged, it + 1)
                        pv_unit(k, n, r, t + 1, it, 8, 18, pT_a, pTs_a, vS_a, False)

            s_unit(0, 0, 0, 0, 8, qS_a[:, 0, :], kS_a, [(q_staged, 1), (k_staged, 1)], False)
            with pe.Fori(0, PAIRS // 2 - 1) as it:
                a_body(it, False)
            a_body(PAIRS // 2 - 1, True)

            def out_linear(u0, kt, ready, hi, lo):
                with pe.Fori(0, KT // 2) as it:
                    for r in range(2):
                        linear(u0 + r, kt, P, it, 2, ready if r == 0 else None, hi, lo)

            def ffn_half(half, u0, ada_b, act_base, hid_base):
                done = 0
                if ada_b is not None:
                    for batch in range(2):
                        for j in range(8):
                            linear(u0 + 8 * batch + j, ready=(act_ready, act_base) if half == 0 and batch + j == 0 else None)
                            ada_step(KT * (ada_b + batch) + j)
                        ada_transpose(ada_b + batch, T_ADA3 + ada_b - 3 + batch)
                    done = 8
                with pe.Fori(0, HT - done) as it:
                    for g in range(2):
                        linear(u0 + 2 * done + g, it=it, per=2,
                               ready=(act_ready, act_base) if g == 0 else None)
                out_linear(u0 + 2 * HT, HT, (hid_ready, hid_base), hid_hi, hid_lo)

            out_linear(U_OA, KT, (act_ready, ACT_OA), act_hi, act_lo)
            norm_sums(1)
            ffn_half(0, U_F0, 3, ACT_N1, 0)
            ffn_half(1, U_F0 + FFN_N, 5, ACT_N1, HT)
            norm_sums(2)

            linear(U_FG, m=16, ready=(act_ready, ACT_N2))
            pe.wait_ge(lfc_in, 16)
            t_use(T_LF)
            for t in range(2):
                last = nc.tensor.transpose(T[0:16, t * P:(t + 1) * P], lfc[:, t, :], ident)
            last.then_inc(t_ready, 1)

            def k_tokens(par, kp, t, it=0, tper=0, per=0):
                pe.wait_ge(lin_free[kp % 2], (per // 2) * it + free_count(kp))
                t_use(t, it, tper)
                for c in range(4):
                    last = nc.tensor.transpose(T[:, c * P:(c + 1) * P], kS_b[:, par, c * P:(c + 1) * P], ident)
                last.then_inc(t_ready, 1)
                t_use(t + 1, it, tper)
                pe.wait_ge(kvc_in[par], 16 * 2 * (per // 8) * it + 32 * KVC_ROUND[kp])
                for c in range(2):
                    nc.tensor.transpose(T[:, (c + 1) * P:(c + 2) * P], kc_b[:, par, c, :], ident)
                nc.tensor.transpose(T[0:NS, 0:P], kS_b[:, par, NP_ + PAST:NK], ident).then_inc(t_ready, 1)

            def v_tokens(par, vp, t, it=0, tper=0, per=0):
                pe.wait_ge(lin_free[vp % 2], (per // 2) * it + free_count(vp))
                for e in range(2):
                    t_use(t + e, it, tper)
                    for c in (range(3) if e == 0 else (3, 4)):
                        w = P if c < 4 else NS
                        last = nc.tensor.transpose(T[0:w, (c % 3) * P:(c % 3 + 1) * P],
                                                   vTb_b[:, c * P:c * P + w], ident)
                    last.then_inc(t_ready, 1)

            linear(U_B)
            linear(U_B + 1)
            pe.wait_ge(lf_dve, LF_DONE)
            t_use(T_LF + 1)
            for t in range(5):
                w = P if t < 4 else NS
                last = nc.tensor.transpose(T[0:w, t * 16:(t + 1) * 16], lb[:, t * P:t * P + w], ident[0:16, 0:16])
            last.then_inc(t_ready, 1)
            linear(U_B + 2)
            k_tokens(0, U_B + 1, T_B0)
            linear(U_B + 3)
            v_tokens(0, U_B + 2, T_B0 + 2)

            def b_ready(u, par, rnd, it, per):
                return [(lin_free[u % 2], (per // 2) * it + free_count(u)),
                        (lin_free[(u + 1) % 2], (per // 2) * it + free_count(u + 1)),
                        (bk_in[par], 32 * it * (per > 0) + 32 * rnd)]

            def b_body(it, last_turn):
                for r in range(2):
                    nxt = not (last_turn and r == 1)
                    for k in range(4):
                        n = 32 + 4 * r + k
                        u = U_B + 4 * (r + 1) + k
                        t = T_B + 13 * r + (0, 3, 5, 9)[k]
                        if not nxt:
                            t = T_B + 13 * r + (0 if k == 0 else 1 + 2 * k)
                        t_unit(k, 0, r, n, t, it, 8, 26, pr_b, ps_b)
                        if not (last_turn and r == 1 and k == 3):
                            k2, r2 = (k + 1) % 4, r + (k == 3)
                            ready = []
                            if k2 == 0:
                                ready = b_ready(U_B + 4 * r2, r2 % 2, 1 + r2 // 2, it, 8)
                                ready.append((t_free, 26 * it + T_B + 13 * r + 9))
                            s_unit(k2, r2 % 2, n + 1, it, 8, qS_b[:, r2 % 2, :], kS_b[:, r2 % 2, :], ready, True)
                        t_unit(k, 1, r, n, t + 1, it, 8, 26, pr_b, ps_b)
                        if nxt:
                            lin_part(u, 0, KT, P, act_hi, act_lo, it, 8)
                        pv_unit(k, n, PAIRS + r, t + 1, it, 8, 26, pT_b, pTs_b, vS_b[:, r, :, :], True)
                        if nxt:
                            lin_part(u, 1, KT, P, act_hi, act_lo, it, 8)
                            if k == 2:
                                k_tokens((r + 1) % 2, u - 1, T_B + 13 * r + 7, it, 26, 8)
                            if k == 3:
                                v_tokens((r + 1) % 2, u - 1, T_B + 13 * r + 11, it, 26, 8)

            s_unit(0, 0, 32, 0, 8, qS_b[:, 0, :], kS_b[:, 0, :],
                   b_ready(U_B, 0, 1, 0, 0) + [(t_free, T_B0 + 2)], True)
            with pe.Fori(0, PAIRS // 2 - 1) as it:
                b_body(it, False)
            b_body(PAIRS // 2 - 1, True)

            out_linear(U_OB, KT, (act_ready, ACT_OB), act_hi, act_lo)
            norm_sums(3)
            ffn_half(0, U_F1, None, ACT_N3, 2 * HT)
            ffn_half(1, U_F1 + FFN_N, None, ACT_N3, 3 * HT)
            norm_sums(4)
            for t in range(5):
                w = P if t < 4 else NS
                for h in range(2):
                    pe.wait_ge(f_done, 4 * KT + 4 * h + 4)
                    t_use(T_Y + 2 * t + h)
                    for j in range(4):
                        last = nc.tensor.transpose(T[0:w, j * P:(j + 1) * P], fo[:, 4 * h + j, t * P:t * P + w], ident)
                    last.then_inc(t_ready, 1)

        @block.scalar
        def _(act):
            A = nc.scalar.activation

            def split_hi(u, n, it=0, per=0):
                act.wait_ge(raw_in[u % 2], 16 * ((per // 2) * it + u // 2 + 1))
                if u >= 2:
                    act.wait_ge(mm_done, per * it + u - 1)
                A(w_hi[:, u % 2, 0:n], w_raw[:, u % 2, 0:n], ACT.Copy).then_inc(whi_done, 1)

            def halves(dst):
                return dst.rearrange("p (h t) -> p h t", h=2)

            act.wait_ge(cs_zero, 1)
            act.wait_ge(t_free, 1)
            A(cs_w[:, :, 0:2], vecs[:, 112:128].rearrange("p (s k) -> p k s", s=2), ACT.Silu).then_inc(cs_done, 1)

            def norm(nz, ready, act_base):
                for kt in range(KT):
                    ready(kt)
                    if kt >= 2:
                        act.wait_ge(ss_done, KT * nz + kt - 1)
                    A(sq[:, kt % 2, :], x[:, kt, :], ACT.Square).then_inc(sq_done, 1)
                act.wait_ge(ss_done, KT * (nz + 1))
                A(halves(root[:, :]), S[:, :, 0:HALF], ACT.Sqrt, scale=1.0 / D, bias=eps[:, 0:1]).then_inc(root_done, 1)
                shift = SHIFT[nz]
                for kt in range(KT):
                    act.wait_ge(y_done, KT * nz + kt + 1)
                    if act_base is not None and kt >= 2:
                        act.wait_ge(act_ready, act_base + kt - 1)
                    dst = fb[:, kt % 2, :] if act_base is not None else fo[:, kt, :]
                    A(dst[:, 0:NP_], yb[:, kt % 2, 0:NP_], ACT.Identity, scale=mulA[:, nz, kt, 0:1],
                      bias=mods[:, shift + kt, 0:1])
                    A(dst[:, NP_:TOK], yb[:, kt % 2, NP_:TOK], ACT.Identity, scale=mulA[:, nz, kt, 1:2],
                      bias=mods[:, shift + kt, 1:2]).then_inc(f_done, 1)

            def ada_evac(b):
                act.wait_ge(ada_used, KT * (b + 1))
                if b >= 1:
                    act.wait_ge(t_ready, T_ADA[b - 1] + 1)
                A(ada_row[:, :], O[:, :], ACT.Copy).then_inc(ada_row_done, 1)

            act.wait_ge(ones_done, 2)
            ada_evac(0)

            def x_loaded_all(kt):
                if kt == 0:
                    act.wait_ge(t_free, T_KC)

            norm(0, x_loaded_all, ACT_N0)

            def raw_evac(u):
                r = rope_of(u)
                act.wait_ge(mm_done, u + 1)
                if r >= 2:
                    act.wait_ge(rope_done, r - 1)
                rows = 64 if u == U_KIW else P
                A(halves(rawb[0:rows, r % 2, :]), lin[0:rows, u % 2, :, 0:HALF], ACT.Copy).then_inc(raw_done, 1)

            def perm_evac(u):
                r = rope_of(u)
                act.wait_ge(perm_done, r + 1)
                rows = 64 if u == U_KIW else P
                A(halves(permb[0:rows, r % 2, :]), lin[0:rows, u % 2, :, 0:HALF], ACT.Copy)\
                    .then_inc(lin_free[u % 2], 1)

            def v_evac(u):
                act.wait_ge(mm_done, u + 1)
                if u == U_V:
                    act.wait_ge(t_ready, T_KIW + 1)
                else:
                    act.wait_ge(t_ready, T_V0 + 2)
                A(halves(vTb[:, :]), lin[:, u % 2, :, 0:HALF], ACT.Copy).then_inc(lin_free[u % 2], 1)

            def k_dup(j):
                act.wait_ge(rope_done, rope_of(U_K + j) + 1)
                for e in range(2):
                    for half in range(2):
                        for c0, c1, d0 in ((0, NP_, 0), (NP_, TOK, NP_ + PAST)):
                            last = A(kT4[64 * half:64 * half + 64, 2 * j + e, d0:d0 + c1 - c0],
                                     kR[64 * e:64 * e + 64, c0:c1], ACT.Copy)
                last.then_inc(kdup_done, 1)

            def token_major_evac(dst, cols, t0):
                act.wait_ge(t_ready, t0 + 1)
                A(dst[:, 0:4, cols], T[:, :].rearrange("p (t c) -> p t c", t=4), ACT.Copy).then_inc(t_free, 1)
                row = 4 if dst is kout else 6
                act.wait_ge(t_ready, t0 + 2)
                A(dst[0:NS, row, cols], T[0:NS, 0:P], ACT.Copy).then_inc(t_free, 1)

            N = KT * P
            split_hi(U_KIW, KT * 72)
            split_hi(U_QI, N)
            raw_evac(U_KIW)
            A(halves(vTb[64:72, :]), lin[64:72, 0, :, 0:HALF], ACT.Copy)
            perm_evac(U_KIW)
            split_hi(U_QI + 1, N)
            raw_evac(U_QI)
            split_hi(U_QI + 2, N)
            perm_evac(U_QI)
            raw_evac(U_QI + 1)
            act.wait_ge(rope_done, 1)
            A(kiT[64:P, 0:NP_], kiT[0:64, 0:NP_], ACT.Copy)
            A(kiT[64:P, NP_ + PAST:NK], kiT[0:64, NP_ + PAST:NK], ACT.Copy).then_inc(kidup_done, 1)
            split_hi(U_QI + 3, N)
            perm_evac(U_QI + 1)
            raw_evac(U_QI + 2)
            act.wait_ge(t_ready, T_KIW + 1)
            Tk = T[:, 0:360].rearrange("p (t c) -> p t c", t=5)
            A(kiout[:, 0:4, :], Tk[:, 0:4, 0:64], ACT.Copy)
            A(wi_t[:, 0:4, :], Tk[:, 0:4, 64:72], ACT.Copy, scale=(NIDX * HD) ** -0.5)
            A(kiout[0:NS, 4, :], Tk[0:NS, 4, 0:64], ACT.Copy)
            A(wi_t[0:NS, 4, :], Tk[0:NS, 4, 64:72], ACT.Copy, scale=(NIDX * HD) ** -0.5).then_inc(t_free, 1)
            act.wait_ge(t_free, T_KIW + 1)
            act.dma_start(o["kidx_p"][0, 0].rearrange("(t p) d -> p t d", p=P), kiout[:, 0:4, :]).then_inc(out_sent, 16)
            act.dma_start(o["kidx_s"][0, 0], kiout[0:NS, 4, :]).then_inc(out_sent, 16)
            split_hi(U_K, N)
            perm_evac(U_QI + 2)
            raw_evac(U_QI + 3)
            split_hi(U_K + 1, N)
            perm_evac(U_QI + 3)
            raw_evac(U_K)

            def idx_relu(n):
                qt = 3 - n // 4
                rows, nk = (P, (qt + 1) * P) if qt else (NS, PAST + NS)
                act.wait_ge(idx_done, n + 1)
                if n >= 1:
                    act.wait_ge(sc_step, 2 * n)
                A(rel[0:rows, :, 0:nk], S[0:rows, :, 0:nk], ACT.Relu).then_inc(rel_done, 1)

            nxt = {0: U_V, 1: U_V + 1, 2: U_Q, 3: U_Q + 1}
            for j in range(4):
                idx_relu(4 * j)
                split_hi(nxt[j], N)
                for e in range(1, 4):
                    idx_relu(4 * j + e)
                if j == 0:
                    perm_evac(U_K)
                    raw_evac(U_K + 1)
                if j == 1:
                    k_dup(0)
                    perm_evac(U_K + 1)
                    token_major_evac(kout, slice(0, P), T_K0)
                    v_evac(U_V)
                if j == 2:
                    k_dup(1)
                    token_major_evac(kout, slice(P, 2 * P), T_K0 + 2)
                    token_major_evac(v4, slice(0, P), T_V0)
                    v_evac(U_V + 1)
                if j == 3:
                    token_major_evac(v4, slice(P, 2 * P), T_V0 + 2)
            act.wait_ge(t_free, T_V0 + 4)
            for name, buf, row in (("a_k", kout, 4), ("a_v", v4, 6)):
                act.dma_start(o[name + "_p"][0, 0].rearrange("(t p) g d -> p t (g d)", p=P), buf[:, 0:4, :])\
                    .then_inc(out_sent, 16)
                act.dma_start(o[name + "_s"][0, 0].rearrange("p g d -> p (g d)"), buf[0:NS, row, :])\
                    .then_inc(out_sent, 16)
            raw_evac(U_Q)
            n = KT
            for j in range(1, PAIRS):
                if j + 1 < PAIRS:
                    split_hi(U_Q + j + 1, N)
                else:
                    split_hi(U_OA, N)
                perm_evac(U_Q + j - 1)
                if n < 2 * KT <= n + ADA_STEPS[j - 1]:
                    ada_evac(1)
                n += ADA_STEPS[j - 1]
                raw_evac(U_Q + j)
            perm_evac(U_Q + PAIRS - 1)
            ada_evac(2)

            def exp_unit(k, n, it, per, pr, ps):
                act.wait_ge(max_done, per * it + n + 1)
                for e in range(2):
                    buf = pr[:, k % 2, e, 0:(k + 1) * P]
                    last = A(buf, buf, ACT.Exp, scale=-1.0, bias=negmax[:, k % 2, e:e + 1],
                             accum_out=rowsum[:, k % 2, e:e + 1])
                if k == 0:
                    last = A(ps[:, :], ps[:, :], ACT.Exp, scale=-1.0, bias=negmax[:, 0, 2:3],
                             accum_out=rowsum[:, 0, 2:3])
                last.then_inc(exp_done, 1)

            def pT_evac(k, t, n, it, per, tper, pT):
                act.wait_ge(t_ready, tper * it + t + 1)
                if n >= 1:
                    act.wait_ge(pv_done, per * it + n)
                if k == 0:
                    A(pT[:, :, 0:P], T[:, 0:2 * P].rearrange("p (e c) -> p e c", e=2), ACT.Copy).then_inc(t_free, 1)
                else:
                    A(pT[:, 0, 0:(k + 1) * P], T[:, 0:(k + 1) * P], ACT.Copy).then_inc(t_free, 1)

            def a_body(it, last_turn):
                for r in range(2):
                    for k in range(4):
                        n = 4 * r + k
                        t = T_A + 9 * r + (0 if k == 0 else 1 + 2 * k)
                        pT_evac(k, t, n, it, 8, 18, pT_a)
                        if not (last_turn and n == 7):
                            exp_unit((k + 1) % 4, n + 1, it, 8, pr_a, ps_a)
                        if k == 0:
                            act.wait_ge(t_ready, 18 * it + t + 3)
                            A(qo[:, ds(2 * it + r, 1), NP_:TOK], T[:, 0:NS].rearrange("p (a c) -> p a c", a=1), ACT.Copy)\
                                .then_inc(t_free, 1)
                        if k == 3:
                            act.wait_ge(pv_done, 8 * it + n + 1)
                            A(qo[:, ds(2 * it + r, 1), 0:NP_], O[:, :].rearrange("p (a c) -> p a c", a=1), ACT.Copy)\
                                .then_inc(o_free, 1)

            exp_unit(0, 0, 0, 8, pr_a, ps_a)
            with act.Fori(0, PAIRS // 2 - 1) as it:
                a_body(it, False)
            a_body(PAIRS // 2 - 1, True)

            def split_o(pairs_done, base):
                act.wait_ge(o_free, pairs_done)
                for kt in range(KT):
                    A(act_hi[:, kt, :], qo[:, kt, :], ACT.Copy).then_inc(acthi_done, 1)

            split_o(PAIRS, ACT_OA)

            def out_stage(u0, n, n_next):
                with act.Fori(0, KT // 2 - 1) as it:
                    for r in range(2):
                        split_hi(u0 + r + 1, n, it, 2)
                split_hi(u0 + KT - 1, n)
                if n_next:
                    split_hi(u0 + KT, n_next)

            def after_out(u0):
                return lambda kt: act.wait_ge(lin_free[(u0 + kt) % 2], free_count(u0 + kt))

            def ffn_half(half, u0, ada_b, hid_base, n_next):
                def tile(j, u, it, per, n2=N):
                    split_hi(u + 1, N, it, per)
                    act.wait_ge(mm_done, per * it + u + 1)
                    if not (isinstance(hid_base, int) and hid_base == 0 and u == U_F0):
                        act.wait_ge(hid_ready, (per // 2) * it + hid_base + j)
                    A(halves(sg[:, :]), lin[:, u % 2, :, 0:HALF], ACT.Silu).then_inc(lin_free[u % 2], 1)
                    split_hi(u + 2, n2, it, per)
                    act.wait_ge(lin_free[(u + 1) % 2], (per // 2) * it + free_count(u + 1))
                    A(hid_hi[:, ds(it + j, 1), :], hf[:, :].rearrange("p (a c) -> p a c", a=1), ACT.Copy)\
                        .then_inc(hidhi_done, 1)

                done = 0
                if ada_b is not None:
                    for batch in range(2):
                        for r in range(4):
                            tile(4 * batch + r, u0 + 8 * batch + 2 * r, 0, 0)
                        ada_evac(ada_b + batch)
                    done = 8
                with act.Fori(0, HT - done - 1) as it:
                    tile(done, u0 + 2 * done, it, 2)
                tile(HT - 1, u0 + 2 * HT - 2, 0, 0, HT * P)
                out_stage(u0 + 2 * HT, HT * P, n_next)

            out_stage(U_OA, N, N)
            act.wait_ge(out_sent, 16 * 6)
            norm(1, after_out(U_OA), ACT_N1)
            ffn_half(0, U_F0, 3, 0, N)
            ffn_half(1, U_F0 + FFN_N, 5, HT, KT * 16)
            norm(2, after_out(U_F0 + 2 * FFN_N - KT), ACT_N2)

            split_hi(U_B, N)
            act.wait_ge(mm_done, U_FG + 1)
            A(halves(zb[:, :]), lin[0:16, U_FG % 2, :, 0:HALF], ACT.Identity, bias=bias_f[:, 0:1])\
                .then_inc(lin_free[U_FG % 2], 1)
            act.wait_ge(lin_free[U_FG % 2], free_count(U_FG))
            A(eb[:, :], zb[:, :], ACT.Abs).then_inc(lf_act, 1)
            act.wait_ge(lf_act, 1)
            A(eb[:, :], eb[:, :], ACT.Exp, scale=-1.0).then_inc(lf_act, 1)
            act.wait_ge(lf_dve, 1)
            A(lb[:, :], ub[:, :], ACT.Ln).then_inc(lf_act, 1)

            def q_evac(par, u, it=0, per=0):
                act.wait_ge(mm_done, per * it + u + 1)
                A(halves(qS_b[:, par, :]), lin[:, u % 2, :, 0:HALF], ACT.Copy).then_inc(lin_free[u % 2], 1)

            def v_evac_b(u, it=0, per=0):
                act.wait_ge(mm_done, per * it + u + 1)
                A(halves(vTb_b[:, :]), lin[:, u % 2, :, 0:HALF], ACT.Copy).then_inc(lin_free[u % 2], 1)

            def g_evac(par, u, it=0, per=0):
                act.wait_ge(mm_done, per * it + u + 1)
                A(halves(gsig[:, par, :]), lin[:, u % 2, :, 0:HALF], ACT.Exp, scale=-1.0).then_inc(lin_free[u % 2], 1)

            def k_tokens_evac(par, pair, t, sent, it=0, tper=0):
                act.wait_ge(t_ready, tper * it + t + 1)
                if sent is not None:
                    act.wait_ge(kv_sent, sent)
                A(kout_b[:, 0:4, :], T[:, :].rearrange("p (t c) -> p t c", t=4), ACT.Copy).then_inc(t_free, 1)
                act.wait_ge(t_ready, tper * it + t + 2)
                A(kout_b[0:NS, 4, :], T[0:NS, 0:P], ACT.Copy)
                A(kS_b[:, par, NP_:NP_ + PAST], T[:, P:3 * P], ACT.Copy).then_inc(t_free, 1)
                act.wait_ge(t_free, tper * it + t + 2)
                cols = ds(pair * P, P)
                act.dma_start(o["b_k_p"][0, 0].rearrange("(t p) h d -> p t (h d)", p=P)[:, :, cols], kout_b[:, 0:4, :])\
                    .then_inc(kv_sent, 16)
                act.dma_start(o["b_k_s"][0, 0].rearrange("p h d -> p (h d)")[:, cols], kout_b[0:NS, 4, :])\
                    .then_inc(kv_sent, 16)

            def v_tokens_evac(par, pair, t, it=0, tper=0):
                act.wait_ge(t_ready, tper * it + t + 1)
                A(vS_b[:, par, 0:3, :], T[:, 0:3 * P].rearrange("p (t c) -> p t c", t=3), ACT.Copy).then_inc(t_free, 1)
                act.wait_ge(t_ready, tper * it + t + 2)
                A(vS_b[:, par, 3, :], T[:, 0:P], ACT.Copy)
                A(vS_b[0:NS, par, 6, :], T[0:NS, P:2 * P], ACT.Copy).then_inc(t_free, 1)
                act.wait_ge(t_free, tper * it + t + 2)
                cols = ds(pair * P, P)
                act.dma_start(o["b_v_p"][0, 0].rearrange("(t p) h d -> p t (h d)", p=P)[:, :, cols],
                              vS_b[:, par, 0:4, :]).then_inc(kv_sent, 16)
                act.dma_start(o["b_v_s"][0, 0].rearrange("p h d -> p (h d)")[:, cols], vS_b[0:NS, par, 6, :])\
                    .then_inc(kv_sent, 16)

            split_hi(U_B + 1, N)
            q_evac(0, U_B)
            split_hi(U_B + 2, N)
            act.wait_ge(t_ready, T_LF + 2)
            A(lf_tok[:, 0:4, :], T[:, 0:64].rearrange("p (t c) -> p t c", t=4), ACT.Copy)
            A(lf_tok[0:NS, 4, :], T[0:NS, 64:80], ACT.Copy).then_inc(t_free, 1)
            act.wait_ge(t_free, T_LF + 2)
            act.dma_start(o["b_lf_p"][0, 0].rearrange("(t p) h -> p t h", p=P), lf_tok[:, 0:4, :]).then_inc(out_sent, 16)
            act.dma_start(o["b_lf_s"][0, 0], lf_tok[0:NS, 4, :]).then_inc(out_sent, 16)
            act.wait_ge(lf_dve, LF_CUM)
            act.dma_start(cum_dram, cum[:, :]).then_inc(cum_out, 16)
            split_hi(U_B + 3, N)
            k_tokens_evac(0, 0, T_B0, None)
            v_evac_b(U_B + 2)
            split_hi(U_B + 4, N)
            g_evac(0, U_B + 3)
            v_tokens_evac(0, 0, T_B0 + 2)
            act.wait_ge(cum_out, 16)
            act.wait_ge(out_sent, 16 * N_OUT_A)

            def b_body(it, last_turn):
                for r in range(2):
                    nxt = not (last_turn and r == 1)
                    for k in range(4):
                        n = 32 + 4 * r + k
                        u = U_B + 4 * (r + 1) + k
                        t = T_B + 13 * r + (0, 3, 5, 9)[k]
                        if not nxt:
                            t = T_B + 13 * r + (0 if k == 0 else 1 + 2 * k)
                        par2 = (r + 1) % 2
                        pair2 = 2 * it + r + 1
                        pT_evac(k, t, n, it, 8, 26, pT_b)
                        if not (last_turn and r == 1 and k == 3):
                            exp_unit((k + 1) % 4, n + 1, it, 8, pr_b, ps_b)
                        if nxt:
                            split_hi(u + 1, N, it, 8)
                            if k == 0:
                                q_evac(par2, u, it, 8)
                            if k == 2:
                                v_evac_b(u, it, 8)
                                k_tokens_evac(par2, pair2, T_B + 13 * r + 7, 64 * (2 * it + r + 1), it, 26)
                            if k == 3:
                                g_evac(par2, u, it, 8)
                                v_tokens_evac(par2, pair2, T_B + 13 * r + 11, it, 26)

            exp_unit(0, 32, 0, 8, pr_b, ps_b)
            with act.Fori(0, PAIRS // 2 - 1) as it:
                b_body(it, False)
            b_body(PAIRS // 2 - 1, True)

            split_o(2 * PAIRS, ACT_OB)
            out_stage(U_OB, N, N)
            act.wait_ge(kv_sent, 16 * 4 * PAIRS)
            norm(3, after_out(U_OB), ACT_N3)
            ffn_half(0, U_F1, None, 2 * HT, N)
            ffn_half(1, U_F1 + FFN_N, None, 3 * HT, 0)
            norm(4, after_out(U_F1 + 2 * FFN_N - KT), None)
            for j in range(10):
                t, h = j // 2, j % 2
                w = P if t < 4 else NS
                act.wait_ge(t_free, T_Y + j + 1)
                dst = o["y_p"][0, t * P:(t + 1) * P, :] if t < 4 else o["y_s"][0]
                act.dma_start(dst[:, h * 512:(h + 1) * 512], y_tok[0:w, j % 2, :]).then_inc(y_sent[j % 2], 16)

        @block.gpsimd
        def _(pool):
            TT, TS, CP = nc.gpsimd.tensor_tensor, nc.gpsimd.tensor_scalar, nc.gpsimd.tensor_copy

            def split_lo(u, n, it=0, per=0):
                pool.wait_ge(whi_done, per * it + u + 1)
                TT(w_lo[:, u % 2, 0:n], w_raw[:, u % 2, 0:n], w_hi[:, u % 2, 0:n].bitcast(F32), ALU.subtract)\
                    .then_inc(wlo_done, 1)

            nc.gpsimd.memset(cs_w[:, :, :], 0.0).then_inc(cs_zero, 1)
            nc.gpsimd.memset(ones[:, :], 1.0).then_inc(ones_done, 1)
            nc.gpsimd.memset(eps[:, :], EPS).then_inc(ones_done, 1)

            def norm(nz):
                for kt in range(KT):
                    pool.wait_ge(f_done, KT * nz + kt + 1)
                    CP(act_hi[:, kt, :], fb[:, kt % 2, :]).then_inc(acthi_done, 1)

            norm(0)
            steps = [0]

            def rope(u):
                r = rope_of(u)
                pool.wait_ge(lin_free[u % 2], free_count(u))
                idx = u < U_K
                cos, sin = tables[:, 2 * idx, :], tables[:, 2 * idx + 1, :]
                rows = 64 if u == U_KIW else P
                if u == U_KIW:
                    pool.wait_ge(const_in, 32)
                raw, par = rawb[0:rows, r % 2, :], permb[0:rows, r % 2, :]
                TT(par, par, sin[0:rows], ALU.mult).then_inc(rope_step, 1)
                TT(raw, raw, cos[0:rows], ALU.mult).then_inc(rope_step, 1)
                steps[0] += 2
                pool.wait_ge(rope_step, steps[0])
                if u == U_KIW:
                    TT(kiT[0:64, 0:NP_], raw[:, 0:NP_], par[:, 0:NP_], ALU.add)
                    TT(kiT[0:64, NP_ + PAST:NK], raw[:, NP_:TOK], par[:, NP_:TOK], ALU.add).then_inc(rope_done, 1)
                    return
                if u < U_K:
                    dst = qiT[:, u - U_QI, :]
                elif u < U_V:
                    dst = kR[:, :]
                    if u == U_K + 1:
                        pool.wait_ge(kdup_done, 1)
                        pool.wait_ge(t_ready, T_K0 + 2)
                else:
                    dst = qo[:, u - U_Q, :]
                TT(dst, raw, par, ALU.add).then_inc(rope_done, 1)

            N = KT * P
            split_lo(U_KIW, KT * 72)
            split_lo(U_QI, N)
            split_lo(U_QI + 1, N)
            rope(U_KIW)
            split_lo(U_QI + 2, N)
            rope(U_QI)
            split_lo(U_QI + 3, N)
            rope(U_QI + 1)
            split_lo(U_K, N)
            rope(U_QI + 2)
            split_lo(U_K + 1, N)
            rope(U_QI + 3)
            split_lo(U_V, N)
            rope(U_K)
            split_lo(U_V + 1, N)
            rope(U_K + 1)
            split_lo(U_Q, N)
            split_lo(U_Q + 1, N)
            for j in range(1, PAIRS):
                split_lo(U_Q + j + 1, N)
                rope(U_Q + j - 1)
            rope(U_Q + PAIRS - 1)

            def stage_q(pair, par, it=0):
                if pair >= 2:
                    pool.wait_ge(s_done, 8 * it + 4 * (pair - 1))
                CP(qS_a[:, par:par + 1, :], qo[:, ds(2 * it + pair, 1), :]).then_inc(q_staged, 1)

            def stage_kv(group, it=0):
                if group >= 1:
                    pool.wait_ge(s_done, 8 * it + 8 * group)
                CP(kS_a[:, :], kT4[:, ds(it + group, 1), :].rearrange("p a c -> p (a c)")).then_inc(k_staged, 1)
                if group >= 1:
                    pool.wait_ge(pv_done, 8 * it + 8 * group)
                cols = ds((it + group) * HD, HD)
                CP(vS_a[:, 0:6, :], v4[:, 0:6, cols])
                CP(vS_a[0:NS, 6, :], v4[0:NS, 6, cols]).then_inc(v_staged, 1)

            def a_body(it, last_turn):
                for r in range(2):
                    for k in range(4):
                        n = 4 * r + k
                        if k == 0 and not (last_turn and r == 1):
                            stage_q(r + 1, (r + 1) % 2, it)
                        if n == 7 and not last_turn:
                            stage_kv(1, it)

            pool.wait_ge(kdup_done, 2)
            pool.wait_ge(sc_step, 33)
            pool.wait_ge(rope_done, rope_of(U_Q + PAIRS - 1) + 1)
            pool.wait_ge(t_ready, T_V0 + 4)
            stage_q(0, 0)
            stage_kv(0)
            with pool.Fori(0, PAIRS // 2 - 1) as it:
                a_body(it, False)
            a_body(PAIRS // 2 - 1, True)

            def out_stage(u0, n, n_next):
                with pool.Fori(0, KT // 2 - 1) as it:
                    for r in range(2):
                        split_lo(u0 + r + 1, n, it, 2)
                split_lo(u0 + KT - 1, n)
                if n_next:
                    split_lo(u0 + KT, n_next)

            def ffn_half(u0, n_next):
                with pool.Fori(0, HT - 1) as it:
                    for g in range(2):
                        split_lo(u0 + g + 1, N, it, 2)
                split_lo(u0 + 2 * HT - 1, N)
                split_lo(u0 + 2 * HT, HT * P)
                out_stage(u0 + 2 * HT, HT * P, n_next)

            out_stage(U_OA, N, N)
            norm(1)
            ffn_half(U_F0, N)
            ffn_half(U_F0 + FFN_N, KT * 16)
            norm(2)
            for c in range(5):
                split_lo(U_B + c, N)

            def b_body(it, last_turn):
                for r in range(2):
                    for k in range(4):
                        if not (last_turn and r == 1):
                            split_lo(U_B + 4 * (r + 1) + k + 1, N, it, 8)

            with pool.Fori(0, PAIRS // 2 - 1) as it:
                b_body(it, False)
            b_body(PAIRS // 2 - 1, True)
            out_stage(U_OB, N, N)
            norm(3)
            ffn_half(U_F1, N)
            ffn_half(U_F1 + FFN_N, 0)

        @block.vector
        def _(dve):
            V = nc.vector
            muls = [0]

            def tick():
                V.memset(cell[:, :], 0.0)

            dve.wait_ge(const_in, 16)
            V.tensor_copy(ident_b[:, :], ident)
            V.tensor_copy(tri_b[:, :], tri)
            dve.wait_ge(t_ready, 1)
            V.tensor_copy(vecs[:, :], T[:, 0:P]).then_inc(t_free, 1)
            dve.wait_ge(t_ready, 2)
            V.tensor_copy(gains[:, :], T[:, 0:40]).then_inc(t_free, 1)
            for t in range(5):
                w = P if t < 4 else NS
                for h in range(2):
                    dve.wait_ge(t_ready, T_X + 2 * t + h + 1)
                    V.tensor_copy(x[:, 4 * h:4 * h + 4, t * P:t * P + w],
                                  T[:, :].rearrange("p (j c) -> p j c", j=4)[:, :, 0:w]).then_inc(t_free, 1)
            for h in range(2):
                dve.wait_ge(t_ready, T_KC + h + 1)
                V.tensor_copy(kT4[:, 2 * h:2 * h + 2, NP_:NP_ + PAST],
                              T[:, :].rearrange("p (g c) -> p g c", g=2)).then_inc(t_free, 1)
            dve.wait_ge(t_ready, T_KIC + 1)
            V.tensor_copy(kiT[:, NP_:NP_ + PAST], T[:, 0:PAST]).then_inc(t_free, 1)

            def ada_mods(b, t):
                dve.wait_ge(t_ready, t + 1)
                V.tensor_tensor(mods[:, 16 * b:16 * b + 16, :].rearrange("p (j c) s -> p j c s", j=4),
                                T[:, :].rearrange("p (c j s) -> p j c s", c=4, j=4)[:, :, :, 0:2],
                                vecs[:, 16 * b:16 * b + 16].rearrange("p (j c a) -> p j c a", j=4, a=1)
                                .broadcast_to([P, 4, 4, 2]), ALU.add).then_inc(t_free, 1)

            def multiplier(nz, t):
                dve.wait_ge(t_free, t + 1)
                V.tensor_scalar(mulA[:, nz, :, :], mods[:, SCALE[nz]:SCALE[nz] + KT, :], 1.0, None, ALU.add)\
                    .then_inc(muls_step, 1)
                muls[0] += 1
                dve.wait_ge(muls_step, muls[0])
                V.tensor_tensor(mulA[:, nz, :, :], mulA[:, nz, :, :],
                                gains[:, GAIN[nz]:GAIN[nz] + KT].rearrange("p (k a) -> p k a", a=1)
                                .broadcast_to([P, KT, 2]), ALU.mult).then_inc(muls_step, 1)
                muls[0] += 1
                dve.wait_ge(muls_step, muls[0])

            def norm(nz, act_base):
                dve.wait_ge(root_done, nz + 1)
                V.reciprocal(rstd[:, :], root[:, :]).then_inc(rstd_done, 1)
                dve.wait_ge(rstd_done, nz + 1)

                def lo(kt):
                    dve.wait_ge(acthi_done, act_base + kt + 1)
                    V.tensor_tensor(act_lo[:, kt, :], fb[:, kt % 2, :], act_hi[:, kt, :].bitcast(F32), ALU.subtract)\
                        .then_inc(act_ready, 1)

                for kt in range(KT):
                    if kt >= 2:
                        dve.wait_ge(f_done, KT * nz + kt - 1)
                    V.tensor_tensor(yb[:, kt % 2, :], x[:, kt, :], rstd[:, :], ALU.mult).then_inc(y_done, 1)
                    if act_base is not None and kt >= 1:
                        lo(kt - 1)
                if act_base is not None:
                    lo(KT - 1)

            ada_mods(0, T_ADA0)
            multiplier(0, T_ADA0)
            norm(0, ACT_N0)

            for n in range(16):
                qt, j = 3 - n // 4, n % 4
                rows, tt, off, nk = (P, qt, OFF[qt], (qt + 1) * P) if qt else (NS, 4, SOFF, PAST + NS)
                dve.wait_ge(rel_done, n + 1)
                dst = sc[0:rows, off:off + nk]
                for e in range(2):
                    w = wi_t[0:rows, tt, 2 * j + e:2 * j + e + 1]
                    if j == 0 and e == 0:
                        V.tensor_scalar(dst, rel[0:rows, 0, 0:nk], w, None, ALU.mult).then_inc(sc_step, 1)
                    else:
                        dve.wait_ge(sc_step, 2 * n + e)
                        V.scalar_tensor_tensor(dst, rel[0:rows, e, 0:nk], w, dst, ALU.mult, ALU.add)\
                            .then_inc(sc_step, 1)
            dve.wait_ge(sc_step, 32)
            for qt in range(1, 4):
                last = V.memset(sc[0:64, OFF[qt] + (qt + 1) * P - 64:OFF[qt] + (qt + 1) * P], FILL)
            last.then_inc(sc_step, 1)
            dve.wait_ge(sc_step, 33)
            tiles = [(P, OFF[qt], (qt + 1) * P) for qt in (3, 2, 1)] + [(NS, SOFF, PAST + NS)]

            def top_round(use, base, it):
                m = len(use)
                for c, (rows, off, nk) in enumerate(use):
                    V.max(top8[0:rows, c, :], sc[0:rows, off:off + nk]).then_inc(top_step, 1)
                dve.wait_ge(top_step, 2 * m * it + base + m)
                tick()
                for c, (rows, off, nk) in enumerate(use):
                    V.match_replace(sc[0:rows, off:off + nk], top8[0:rows, c, :], sc[0:rows, off:off + nk], TAKEN)\
                        .then_inc(top_step, 1)
                dve.wait_ge(top_step, 2 * m * it + base + 2 * m)

            with dve.Fori(0, TOPK_S // 8) as it:
                top_round(tiles, 0, it)
            with dve.Fori(0, (TOPK_P - TOPK_S) // 8) as it:
                top_round(tiles[:3], 8 * (TOPK_S // 8), it)
            V.tensor_scalar(sc[:, P:SOFF], sc[:, P:SOFF], TAKEN, NEG, ALU.not_equal, ALU.mult)
            V.memset(sc[:, 0:P], 0.0).then_inc(mask_done, 1)
            V.tensor_scalar(sc[0:NS, SOFF:], sc[0:NS, SOFF:], TAKEN, NEG, ALU.not_equal, ALU.mult).then_inc(mask_done, 1)
            dve.wait_ge(mask_done, 2)
            V.memset(sc[0:64, 64:P], NEG)
            V.tensor_copy(sc[64:P, SOFF:], sc[0:64, SOFF:]).then_inc(mask_done, 1)
            dve.wait_ge(mask_done, 3)

            def max_unit(k, n, it, per, pr, ps, bias, bias_s):
                dve.wait_ge(s_done, per * it + n + 1)
                if n >= 2:
                    dve.wait_ge(pv_done, per * it + n - 1)
                tick()
                nk, c0 = (k + 1) * P, 384 if k == 0 else 0

                def one(out, in0, in1, acc):
                    return V.tensor_tensor_reduce(out=out, in0=in0, in1=in1, scale=-QSCALE, scalar=3.4e38,
                                                  op0=ALU.add, op1=ALU.min, accum_out=acc)

                if k == 0:
                    for e in range(2):
                        r = slice(64 * e, 64 * e + 64)
                        one(ps[r, :], S[r, e, 0:PAST + NS], bias_s(e, r), negmax[r, 0, 2:3])
                for e in range(2):
                    last = one(pr[:, k % 2, e, 0:nk], S[:, e, c0:c0 + nk], bias(e, k, nk), negmax[:, k % 2, e:e + 1])
                last.then_inc(max_done, 1)

            def norm_unit(k, n, it, per, pr, ps):
                dve.wait_ge(exp_done, per * it + n + 1)
                w = 3 if k == 0 else 2
                V.reciprocal(rinv[:, k % 2, 0:w], rowsum[:, k % 2, 0:w]).then_inc(rinv_done, 1)
                dve.wait_ge(rinv_done, per * it + n + 1)
                for e in range(2):
                    buf = pr[:, k % 2, e, 0:(k + 1) * P]
                    last = V.tensor_scalar(buf, buf, rinv[:, k % 2, e:e + 1], None, ALU.mult)
                if k == 0:
                    last = V.tensor_scalar(ps[:, :], ps[:, :], rinv[:, 0, 2:3], None, ALU.mult)
                last.then_inc(norm_done, 1)

            def pT_evac(k, t, n, it, per, tper, pT, pTs):
                dve.wait_ge(t_ready, tper * it + t + 1)
                if n >= 1:
                    dve.wait_ge(pv_done, per * it + n)
                if k == 0:
                    V.tensor_copy(pTs[:, 0:2, :], T[:, 0:2 * P].rearrange("p (b c) -> p b c", b=2))
                    V.tensor_copy(pTs[0:NS, 2, :], T[0:NS, 2 * P:3 * P]).then_inc(t_free, 1)
                else:
                    V.tensor_copy(pT[:, 1, 0:(k + 1) * P], T[:, 0:(k + 1) * P]).then_inc(t_free, 1)

            def bias_a(e, k, nk):
                return sc[:, OFF[k]:OFF[k] + nk]

            def bias_as(e, r):
                return sc[r, SOFF:]

            def a_body(it, last_turn):
                for r in range(2):
                    for k in range(4):
                        n = 4 * r + k
                        t = T_A + 9 * r + (0 if k == 0 else 1 + 2 * k)
                        if not (last_turn and n == 7):
                            max_unit((k + 1) % 4, n + 1, it, 8, pr_a, ps_a, bias_a, bias_as)
                        pT_evac(k, t + 1, n, it, 8, 18, pT_a, pTs_a)
                        if not (last_turn and n == 7):
                            norm_unit((k + 1) % 4, n + 1, it, 8, pr_a, ps_a)

            ada_mods(1, T_ADA1)
            ada_mods(2, T_ADA2)
            multiplier(1, T_ADA2)
            max_unit(0, 0, 0, 8, pr_a, ps_a, bias_a, bias_as)
            norm_unit(0, 0, 0, 8, pr_a, ps_a)
            with dve.Fori(0, PAIRS // 2 - 1) as it:
                a_body(it, False)
            a_body(PAIRS // 2 - 1, True)

            def split_o(base):
                for kt in range(KT):
                    dve.wait_ge(acthi_done, base + kt + 1)
                    V.tensor_tensor(act_lo[:, kt, :], qo[:, kt, :], act_hi[:, kt, :].bitcast(F32), ALU.subtract)\
                        .then_inc(act_ready, 1)

            def residual(u0, gate):
                with dve.Fori(0, KT // 2) as it:
                    for r in range(2):
                        u = u0 + r
                        m = 2 * it + r
                        dve.wait_ge(mm_done, 2 * it + u + 1)
                        for h, c0, c1, st in ((0, 0, HALF, 0), (1, HALF, NP_, 0), (1, NP_, TOK, 1)):
                            dst = x[:, ds(m, 1), c0:c1].rearrange("p a c -> p (a c)")
                            last = V.scalar_tensor_tensor(dst, lin[:, u % 2, h, c0 - h * HALF:c1 - h * HALF],
                                                          mods[:, ds(m + gate, 1), st:st + 1].rearrange("p a c -> p (a c)"),
                                                          dst, ALU.mult, ALU.add)
                        last.then_inc(lin_free[u % 2], 1)

            def ffn_half(u0, ada_b, hid_base, gate):
                def tile(j, u, it, per):
                    dve.wait_ge(mm_done, per * it + u + 2)
                    dve.wait_ge(lin_free[u % 2], (per // 2) * it + free_count(u))
                    V.tensor_tensor(hf[:, :].rearrange("p (h t) -> p h t", h=2), sg[:, :].rearrange("p (h t) -> p h t", h=2),
                                    lin[:, (u + 1) % 2, :, 0:HALF], ALU.mult).then_inc(lin_free[(u + 1) % 2], 1)
                    dve.wait_ge(hidhi_done, (per // 2) * it + hid_base + j + 1)
                    V.tensor_tensor(hid_lo[:, ds(it + j, 1), :].rearrange("p a c -> p (a c)"), hf[:, :],
                                    hid_hi[:, ds(it + j, 1), :].rearrange("p a c -> p (a c)").bitcast(F32), ALU.subtract)\
                        .then_inc(hid_ready, 1)

                done = 0
                if ada_b is not None:
                    for batch in range(2):
                        for r in range(4):
                            tile(4 * batch + r, u0 + 8 * batch + 2 * r, 0, 0)
                        ada_mods(ada_b + batch, T_ADA[ada_b + batch])
                    done = 8
                with dve.Fori(0, HT - done) as it:
                    tile(done, u0 + 2 * done, it, 2)
                residual(u0 + 2 * HT, gate)

            split_o(ACT_OA)
            residual(U_OA, 16)
            norm(1, ACT_N1)
            ffn_half(U_F0, 3, 0, 40)
            ffn_half(U_F0 + FFN_N, 5, HT, 40)
            for nz, bt in ((2, 3), (3, 5), (4, 6)):
                multiplier(nz, T_ADA[bt])
            norm(2, ACT_N2)

            steps = [0]

            def chain(ins):
                ins.then_inc(lf_dve, 1)
                steps[0] += 1
                dve.wait_ge(lf_dve, steps[0])

            dve.wait_ge(lf_act, 2)
            chain(V.tensor_scalar(ub[:, :], eb[:, :], 1.0, None, ALU.add))
            chain(V.memset(one_row[:, :], 1.0))
            dve.wait_ge(lf_act, 3)
            chain(V.tensor_scalar(ub[:, :], ub[:, :], -1.0, None, ALU.add))
            chain(V.tensor_tensor(lb[:, :], lb[:, :], eb[:, :], ALU.mult))
            chain(V.scalar_tensor_tensor(lb[:, :], ub[:, :], 0.0, lb[:, :], ALU.is_equal, ALU.add))
            chain(V.scalar_tensor_tensor(ub[:, :], ub[:, :], 0.0, ub[:, :], ALU.is_equal, ALU.add))
            chain(V.reciprocal(ub[:, :], ub[:, :]))
            chain(V.tensor_tensor(lb[:, :], lb[:, :], ub[:, :], ALU.mult))
            chain(V.scalar_tensor_tensor(ub[:, :], lb[:, :], 1.0, eb[:, :], ALU.is_equal, ALU.mult))
            chain(V.scalar_tensor_tensor(eb[:, :], lb[:, :], 1.0, lb[:, :], ALU.not_equal, ALU.mult))
            chain(V.tensor_tensor(eb[:, :], eb[:, :], ub[:, :], ALU.add))
            chain(V.scalar_tensor_tensor(lb[:, :], zb[:, :], 0.0, eb[:, :], ALU.min, ALU.subtract))
            assert steps[0] == LF_DONE
            dve.wait_ge(t_ready, T_LF + 1)
            V.tensor_copy(lfs[:, 0:PAST], T[0:16, 0:PAST]).then_inc(t_free, 1)
            chain(V.tensor_copy(lfs[:, PAST:], lb[:, NP_:TOK]))
            dve.wait_ge(t_free, T_LF + 1)
            chain(V.tensor_tensor_scan(cum[:, 0:NP_], one_row[:, 0:NP_], lb[:, 0:NP_], 0.0, ALU.mult, ALU.add))
            chain(V.tensor_tensor_scan(cum[:, NP_:], one_row[:, 0:PAST + NS], lfs[:, :], 0.0, ALU.mult, ALU.add))
            chain(V.tensor_scalar(cum[:, :], cum[:, :], -1.0 / QSCALE, None, ALU.mult))
            assert steps[0] == LF_CUM

            def k_evac(par, u, it=0, per=0):
                dve.wait_ge(mm_done, per * it + u + 1)
                V.tensor_copy(kS_b[:, par, 0:HALF], lin[:, u % 2, 0, 0:HALF])
                V.tensor_copy(kS_b[:, par, HALF:NP_], lin[:, u % 2, 1, 0:NP_ - HALF])
                V.tensor_copy(kS_b[:, par, NP_ + PAST:NK], lin[:, u % 2, 1, NP_ - HALF:HALF])\
                    .then_inc(lin_free[u % 2], 1)

            def gate(par, u, step, it=0, per=0):
                dve.wait_ge(lin_free[u % 2], (per // 2) * it + free_count(u))
                V.tensor_scalar(gsig[:, par, :], gsig[:, par, :], 1.0, None, ALU.add).then_inc(gsig_step, 1)
                dve.wait_ge(gsig_step, (per // 2) // 2 * 2 * it + step + 1)
                V.reciprocal(gsig[:, par, :], gsig[:, par, :]).then_inc(gsig_step, 1)

            k_evac(0, U_B + 1)
            gate(0, U_B + 3, 0)

            def bias_b(par):
                return lambda e, k, nk: bk[:, par, e, 0:nk]

            def bias_bs(par):
                return lambda e, r: bk[r, par, e, NP_:NK]

            def b_body(it, last_turn):
                for r in range(2):
                    nxt = not (last_turn and r == 1)
                    for k in range(4):
                        n = 32 + 4 * r + k
                        u = U_B + 4 * (r + 1) + k
                        t = T_B + 13 * r + (0, 3, 5, 9)[k]
                        if not nxt:
                            t = T_B + 13 * r + (0 if k == 0 else 1 + 2 * k)
                        par2 = (r + 1) % 2
                        if not (last_turn and r == 1 and k == 3):
                            p2 = (r + (k == 3)) % 2
                            max_unit((k + 1) % 4, n + 1, it, 8, pr_b, ps_b, bias_b(p2), bias_bs(p2))
                        pT_evac(k, t + 1, n, it, 8, 26, pT_b, pTs_b)
                        if not (last_turn and r == 1 and k == 3):
                            norm_unit((k + 1) % 4, n + 1, it, 8, pr_b, ps_b)
                        pair = 2 * it + r
                        if k == 0:
                            dve.wait_ge(gsig_step, 4 * it + 2 * r + 2)
                            dve.wait_ge(t_ready, 26 * it + t + 3)
                            V.tensor_tensor(qo[:, ds(pair, 1), NP_:TOK].rearrange("p a c -> p (a c)"), T[:, 0:NS],
                                            gsig[:, r, NP_:TOK], ALU.mult).then_inc(t_free, 1)
                        if k == 3:
                            dve.wait_ge(pv_done, 8 * it + n + 1)
                            V.tensor_tensor(qo[:, ds(pair, 1), 0:NP_].rearrange("p a c -> p (a c)"), O[:, :],
                                            gsig[:, r, 0:NP_], ALU.mult).then_inc(o_free, 1)
                        if nxt and k == 1:
                            k_evac(par2, u, it, 8)
                        if nxt and k == 3:
                            gate(par2, u, 2 * (r + 1), it, 8)

            dve.wait_ge(bk_in[0], 32)
            dve.wait_ge(out_sent, 16 * N_OUT_A)
            max_unit(0, 32, 0, 8, pr_b, ps_b, bias_b(0), bias_bs(0))
            norm_unit(0, 32, 0, 8, pr_b, ps_b)
            with dve.Fori(0, PAIRS // 2 - 1) as it:
                b_body(it, False)
            b_body(PAIRS // 2 - 1, True)

            split_o(ACT_OB)
            residual(U_OB, 64)
            norm(3, ACT_N3)
            ffn_half(U_F1, None, 2 * HT, 88)
            ffn_half(U_F1 + FFN_N, None, 3 * HT, 88)
            norm(4, None)
            for j in range(10):
                w = P if j < 8 else NS
                dve.wait_ge(t_ready, T_Y + j + 1)
                if j >= 2:
                    dve.wait_ge(y_sent[j % 2], 16 * (j // 2))
                V.tensor_copy(y_tok[0:w, j % 2, :], T[0:w, :]).then_inc(t_free, 1)


ADA_STEPS = [2, 2, 2, 2, 3, 3, 2]
T_ADA = [T_ADA0, T_ADA1, T_ADA2, T_ADA3, T_ADA3 + 1, T_ADA3 + 2, T_ADA3 + 3]
SHIFT = [0, 24, 48, 72, 96]
SCALE = [8, 32, 56, 80, 104]
GAIN = [0, 16, 8, 24, 32]
N_OUT_A = 8
LF_DONE, LF_CUM = 12, 16
KVC_ROUND = {U_B + 1: 1, U_B + 5: 1, U_B + 9: 2}

_INS = ["x_prompt", "x_sample", "cache_a_k", "cache_a_v", "cache_a_kidx", "cache_b_k", "cache_b_v", "cache_b_logf",
        "c_prompt", "c_sample", "w_ada", "b_ada", "g_mix", "g_ffn", "w_in_a", "w_out_a", "w_in_b", "b_forget",
        "w_out_b", "w_ffn_in", "w_ffn_out", "w_ada_final", "b_ada_final", "g_final"]
_OUTS = [("y_p", (1, 512, 1024)), ("y_s", (1, 64, 1024)),
         ("a_k_p", (1, 1, 512, 4, 64)), ("a_v_p", (1, 1, 512, 4, 64)), ("kidx_p", (1, 1, 512, 64)),
         ("b_k_p", (1, 1, 512, 16, 64)), ("b_v_p", (1, 1, 512, 16, 64)), ("b_lf_p", (1, 1, 512, 16)),
         ("a_k_s", (1, 1, 64, 4, 64)), ("a_v_s", (1, 1, 64, 4, 64)), ("kidx_s", (1, 1, 64, 64)),
         ("b_k_s", (1, 1, 64, 16, 64)), ("b_v_s", (1, 1, 64, 16, 64)), ("b_lf_s", (1, 1, 64, 16))]


def kernel(**inputs):
    import concourse.bacc as _bacc
    from concourse.bass_utils import run_bass_kernel_spmd as _run

    nc = _bacc.Bacc("TRN2", target_bir_lowering=False, num_devices=1)
    arrays, ins, outs = {}, {}, {}
    for name in _INS:
        arr = np.ascontiguousarray(inputs[name])
        arrays[f"in_{name}"] = arr
        ins[name] = nc.dram_tensor(f"in_{name}", arr.shape, mybir.dt.from_np(arr.dtype), kind="ExternalInput").ap()
    consts = host_constants()
    arrays["in_consts"] = consts
    ins["consts"] = nc.dram_tensor("in_consts", consts.shape, F32, kind="ExternalInput").ap()
    for name, shape in _OUTS:
        outs[name] = nc.dram_tensor(f"out_{name}", shape, F32, kind="ExternalOutput").ap()
    encoder_step(nc, ins, outs)
    r = _run(nc, [arrays], core_ids=[0])
    return tuple(r.results[0][f"out_{name}"] for name, _ in _OUTS)
```

```python
from contextlib import ExitStack

import numpy as np
import concourse.bass as bass
from concourse import mybir
from concourse.alu_op_type import AluOpType as ALU

F32 = mybir.dt.float32
F32R = mybir.dt.float32r
BF16 = mybir.dt.bfloat16
ACT = mybir.ActivationFunctionType
ds = bass.ds

P = 128
D = 1024
NP_, NS = 512, 64
TOK = NP_ + NS
HALF = TOK // 2
PAST = 256
NK = NP_ + PAST + NS
HD = 64
KT = D // P
NQT = NP_ // P
PAIRS = 8
NG = 4
DFF = 2816
HT = DFF // P // 2
NIDX = 8
TOPK_P, TOPK_S = 128, 80
THETA, EPS = 10000.0, 1e-6
NEG = -1e30
FILL, TAKEN = -3.0e38, -3.4e38
WCOL = HT * P
QSCALE = HD ** -0.5
PR = [0, 256, 768, 1536, 2560]
OFF = [0, 128, 384, 768]
SOFF = 1280

U_KIW = 0
U_QI = 1
U_K = 5
U_V = 7
U_Q = 9
U_OA = U_Q + PAIRS
U_F0 = U_OA + KT
FFN_N = 2 * HT + KT
U_FG = U_F0 + 2 * FFN_N
U_B = U_FG + 1
U_OB = U_B + 4 * PAIRS
U_F1 = U_OB + KT

T_ROWS, T_X, T_KC, T_KIC, T_ADA0 = 0, 2, 12, 14, 15
T_KIW = 16
T_K0, T_V0 = 17, 21
T_ADA1 = 25
T_ADA2 = 26
T_A = 27
T_LF = T_A + 9 * PAIRS // 2
T_B0 = T_LF + 1
T_LFO = T_B0 + 2
T_B = T_B0 + 5

ACT_N0, ACT_N1, ACT_N2, ACT_OB, ACT_N3 = (KT * i for i in range(5))


def rope_of(u):
    return u if u < U_V else u - 2


def host_constants():
    pos = np.concatenate([np.arange(NP_), PAST + np.arange(NS)]).astype(np.float32)
    ident = np.eye(P, dtype=np.float32)
    tri = np.where(np.arange(P)[None, :] <= np.arange(P)[:, None], 0.0, NEG).astype(np.float32)
    out = [ident, tri]
    tables = []
    for half in (32, 16):
        perm = np.zeros((P, P), np.float32)
        cos = np.ones((P, TOK), np.float32)
        sin = np.zeros((P, TOK), np.float32)
        inv = (np.float32(THETA) ** (-np.arange(half, dtype=np.float32) / np.float32(half))).astype(np.float32)
        ang = (pos[:, None] * inv[None, :]).astype(np.float32)
        for h in range(2):
            for d in range(2 * half):
                row = 64 * h + d
                first = d < half
                perm[row + half if first else row - half, row] = 1.0
                cos[row] = np.cos(ang[:, d % half])
                sin[row] = np.sin(ang[:, d % half]) * (-1.0 if first else 1.0)
        out.append(perm)
        tables += [cos, sin]
    return np.concatenate(out + tables, axis=1).astype(np.float32)


NCONST = 4 * P


def encoder_step(nc, i, o):
    ctx = ExitStack()
    with ctx:
        def sem(name):
            return ctx.enter_context(nc.semaphore(name))

        def sb(name, shape, dt=F32, scope=ctx):
            return scope.enter_context(nc.sbuf_tensor(name, shape, dt))

        x = sb("x", [P, KT, TOK])
        act_hi = sb("act_hi", [P, KT, TOK], F32R)
        act_lo = sb("act_lo", [P, KT, TOK], F32R)
        w_raw = sb("w_raw", [P, 2, WCOL])
        w_hi = sb("w_hi", [P, 2, WCOL], F32R)
        w_lo = sb("w_lo", [P, 2, WCOL], F32R)
        ada_raw = sb("ada_raw", [P, 2, 2048])
        consts = sb("consts", [P, NCONST])
        ident, tri = consts[:, 0:P], consts[:, P:2 * P]
        perm_q, perm_i = consts[:, 2 * P:3 * P], consts[:, 3 * P:4 * P]
        ident_b = sb("ident_b", [P, P], BF16)
        tri_b = sb("tri_b", [P, P], BF16)
        ones = sb("ones", [P, P])
        vecs = sb("vecs", [P, P])
        gains = sb("gains", [P, 40])
        cs_w = sb("cs_w", [P, KT, 32])
        ada_row = sb("ada_row", [P, 512])
        mods = sb("mods", [P, 112, 2])
        mulA = sb("mulA", [P, 5, KT, 2])
        bias_f = sb("bias_f", [16, 1])
        negmax = sb("negmax", [P, 4, 3])
        rowsum = sb("rowsum", [P, 4, 3])
        rinv = sb("rinv", [P, 4, 3])
        top8 = sb("top8", [P, 4, 8])
        eps = sb("eps", [P, 1])
        cell = sb("cell", [P, 9])

        s = ExitStack()
        rows1 = sb("rows1", [P, P], scope=s)
        rows2 = sb("rows2", [40, P], scope=s)
        x_in = sb("x_in", [P, 5, D], scope=s)
        s.close()
        s = ExitStack()
        fo = sb("fo", [P, KT, TOK], scope=s)
        y_tok = sb("y_tok", [P, 10, 512], scope=s)
        sb("norm_pad", [P, 2 * HT * TOK + 2 * TOK - KT * TOK - 10 * 512], scope=s)
        sq = sb("sq", [P, 2, TOK], scope=s)
        ssq = sb("ssq", [P, TOK], scope=s)
        root = sb("root", [P, 6], scope=s)
        rstd = sb("rstd", [P, 5], scope=s)
        s.close()
        s = ExitStack()
        hid_hi = sb("hid_hi", [P, HT, TOK], F32R, scope=s)
        hid_lo = sb("hid_lo", [P, HT, TOK], F32R, scope=s)
        sg = sb("sg", [P, TOK], scope=s)
        hf = sb("hf", [P, TOK], scope=s)
        s.close()
        qo = sb("qo", [P, PAIRS, TOK])
        a = ExitStack()
        kT4 = sb("kT4", [P, NG, NK], scope=a)
        kiT = sb("kiT", [P, NK], scope=a)
        b = ExitStack()
        ada0_mid = sb("ada0_mid", [P, 2048], scope=b)
        b.close()
        v4 = sb("v4", [P, 7, NG * HD], scope=a)
        sc = sb("sc", [P, SOFF + PAST + NS], scope=a)
        b = ExitStack()
        kout = sb("kout", [P, 5, NG * HD], scope=b)
        kiout = sb("kiout", [P, 5, HD], scope=b)
        b.close()
        b = ExitStack()
        kc_in = sb("kc_in", [P, 2, NG, 2, HD], scope=b)
        kic_in = sb("kic_in", [P, 2, 2, HD], scope=b)
        b.close()
        sb("kout_pad", [P, 5 * NG * HD + 5 * HD], scope=a)
        b = ExitStack()
        sb("ada0_pad", [P, 2048], scope=b)
        ada0_tail = sb("ada0_tail", [P, 3, 2048], scope=b)
        b.close()
        b = ExitStack()
        tables = sb("tables", [P, 4, TOK], scope=b)
        rawb = sb("rawb", [P, 2, TOK], scope=b)
        permb = sb("permb", [P, 2, TOK], scope=b)
        vTb = sb("vTb", [P, TOK], scope=b)
        kR = sb("kR", [P, TOK], scope=b)
        qiT = sb("qiT", [P, 4, TOK], scope=b)
        rel = sb("rel", [P, 2, 512], scope=b)
        wi_t = sb("wi_t", [P, 5, NIDX], scope=b)
        b.close()
        b = ExitStack()
        qS_a = sb("qS_a", [P, 2, TOK], scope=b)
        kS_a = sb("kS_a", [P, NK], scope=b)
        vS_a = sb("vS_a", [P, 7, HD], scope=b)
        pr_a = sb("pr_a", [P, PR[4]], scope=b)
        ps_a = sb("ps_a", [P, PAST + NS], scope=b)
        pT_a = sb("pT_a", [P, 2, 512], scope=b)
        pTs_a = sb("pTs_a", [P, 3, P], scope=b)
        ada_raw2 = sb("ada_raw2", [P, 2048], scope=b)
        b.close()
        a.close()
        b = ExitStack()
        fw = ExitStack()
        zb = sb("zb", [16, TOK], scope=fw)
        eb = sb("eb", [16, TOK], scope=fw)
        ub = sb("ub", [16, TOK], scope=fw)
        lb = sb("lb", [16, TOK], scope=fw)
        lfs = sb("lfs", [16, PAST + NS], scope=fw)
        cum = sb("cum", [16, NK], scope=fw)
        one_row = sb("one_row", [16, 512], scope=fw)
        lfc = sb("lfc", [P, 2, 16], scope=fw)
        lf_tok = sb("lf_tok", [P, 5, 16], scope=fw)
        fw.close()
        pr_b = sb("pr_b", [P, PR[4]], scope=b)
        ps_b = sb("ps_b", [P, PAST + NS], scope=b)
        pT_b = sb("pT_b", [P, 2, 512], scope=b)
        pTs_b = sb("pTs_b", [P, 3, P], scope=b)
        sb("forget_pad", [P, 64], scope=b)
        qS_b = sb("qS_b", [P, 2, TOK], scope=b)
        kS_b = sb("kS_b", [P, 2, NK], scope=b)
        vS_b = sb("vS_b", [P, 2, 7, P], scope=b)
        vTb_b = sb("vTb_b", [P, TOK], scope=b)
        kout_b = sb("kout_b", [P, 5, P], scope=b)
        kc_b = sb("kc_b", [P, 2, 2, P], scope=b)
        bk = sb("bk", [P, 2, 2, NK], scope=b)
        gsig = sb("gsig", [P, 2, TOK], scope=b)
        b.close()

        lin = ctx.enter_context(nc.psum_tensor("lin", [P, 2, 2, 512], F32))
        S = ctx.enter_context(nc.psum_tensor("S", [P, 2, 512], F32))
        T = ctx.enter_context(nc.psum_tensor("T", [P, 512], F32))
        O = ctx.enter_context(nc.psum_tensor("O", [P, 512], F32))
        y_bank = [T[:, :], O[:, :], lin[:, 0, 0, :], lin[:, 0, 1, :], lin[:, 1, 0, :], lin[:, 1, 1, :]]
        S2, T2, adaO = lin[:, 0, :, :], lin[:, 1, 0, :], lin[:, 1, 1, :]
        cum_dram = nc.dram_tensor("cum_dram", [16, NK], F32, kind="Internal").ap()

        const_in = sem("const_in")
        rows_in = sem("rows_in")
        x_loaded = [sem(f"x_loaded{t}") for t in range(5)]
        cache_in = sem("cache_in")
        raw_in = [sem("raw_in0"), sem("raw_in1")]
        whi_done, wlo_done = sem("whi_done"), sem("wlo_done")
        mm_done = sem("mm_done")
        lin_free = [sem("lin_free0"), sem("lin_free1")]
        ada0_in = [sem(f"ada0_in{kt}") for kt in range(KT)]
        ada_in = [sem("ada_in0"), sem("ada_in1"), sem("ada_in2")]
        ada_used, ada_row_done = sem("ada_used"), sem("ada_row_done")
        cs_zero, cs_done, ones_done = sem("cs_zero"), sem("cs_done"), sem("ones_done")
        t_ready, t_free = sem("t_ready"), sem("t_free")
        muls_step = sem("muls_step")
        sq_done, ssq_done, ss_done, root_done = sem("sq_done"), sem("ssq_done"), sem("ss_done"), sem("root_done")
        rstd_done, rstd_spread = sem("rstd_done"), sem("rstd_spread")
        y_done, f_done, acthi_done, act_ready = sem("y_done"), sem("f_done"), sem("acthi_done"), sem("act_ready")
        raw_done, perm_done, rope_step, rope_done = sem("raw_done"), sem("perm_done"), sem("rope_step"), sem("rope_done")
        ropev_step = sem("ropev_step")
        kdup_done, kidup_done = sem("kdup_done"), sem("kidup_done")
        idx_done, rel_done, sc_step = sem("idx_done"), sem("rel_done"), sem("sc_step")
        top_step, mask_done = sem("top_step"), sem("mask_done")
        out_sent, kv_sent = sem("out_sent"), sem("kv_sent")
        q_staged, k_staged, v_staged = sem("q_staged"), sem("k_staged"), sem("v_staged")
        t2_ready, t2_free = sem("t2_ready"), sem("t2_free")
        so_ready, so_free, ohi_done, olo_done = sem("so_ready"), sem("so_free"), sem("ohi_done"), sem("olo_done")
        s_done, max_done, exp_done, rinv_done, norm_done = (
            sem("s_done"), sem("max_done"), sem("exp_done"), sem("rinv_done"), sem("norm_done"))
        pv_done, o_free = sem("pv_done"), sem("o_free")
        hidhi_done, hid_ready, silu_done = sem("hidhi_done"), sem("hid_ready"), sem("silu_done")
        z_done, lf_act, lf_dve = sem("z_done"), sem("lf_act"), sem("lf_dve")
        cum_out = sem("cum_out")
        bk_in = [sem("bk_in0"), sem("bk_in1")]
        kvc_in = [sem("kvc_in0"), sem("kvc_in1")]
        lfc_in = sem("lfc_in")
        gsig_step = sem("gsig_step")
        y_ready, y_sent = sem("y_ready"), sem("y_sent")
        y_free = [sem("y_free0"), sem("y_free1")]

        block = ctx.enter_context(nc.Block())

        def ada0_slot(kt):
            return ada0_mid[:, :] if kt == 2 else ada0_tail[:, kt - 3, :] if 3 <= kt < 6 else ada_raw[:, kt % 2, :]

        def ada_place(j):
            return (ada_raw2[:, :] if j % 3 == 2 else ada_raw[:, j % 3, :]), (2 if j % 3 == 2 else 3)

        def probs(pr, k, e):
            return pr[:, PR[k] + e * (k + 1) * P:PR[k] + (e + 1) * (k + 1) * P]

        def free_count(u):
            return u // 2 + 1

        @block.sync
        def _(sp):
            sp.dma_start(consts[:, :], i["consts"][:, 0:NCONST]).then_inc(const_in, 16)
            for t in range(2):
                sp.dma_start(x_in[:, t, :], i["x_prompt"][0, t * P:(t + 1) * P, :]).then_inc(x_loaded[t], 16)
            sp.dma_start(rows1[0:96, :], i["b_ada"].rearrange("l (r p) -> (l r) p", p=P)).then_inc(rows_in, 16)
            sp.dma_start(rows1[96:112, :], i["b_ada_final"].rearrange("(r p) -> r p", p=P)).then_inc(rows_in, 16)
            sp.dma_start(rows1[112:120, :], i["c_prompt"].rearrange("b (r p) -> (b r) p", p=P)).then_inc(rows_in, 16)
            sp.dma_start(rows1[120:128, :], i["c_sample"].rearrange("b (r p) -> (b r) p", p=P)).then_inc(rows_in, 16)
            sp.dma_start(rows2[0:16, :], i["g_mix"].rearrange("l (r p) -> (l r) p", p=P)).then_inc(rows_in, 16)
            sp.dma_start(rows2[16:32, :], i["g_ffn"].rearrange("l (r p) -> (l r) p", p=P)).then_inc(rows_in, 16)
            sp.dma_start(rows2[32:40, :], i["g_final"].rearrange("(r p) -> r p", p=P)).then_inc(rows_in, 16)
            sp.dma_start(bias_f[:, :], i["b_forget"].rearrange("l n -> n l")).then_inc(rows_in, 16)

            def ada_load(n, src):
                sp.wait_ge(ada_used, n - 1)
                sp.dma_start(ada_raw[:, n % 2, :], src).then_inc(ada_in[n % 2], 16)

            def ada_src(b, kt):
                rows = slice(kt * P, (kt + 1) * P)
                if b == 6:
                    return i["w_ada_final"][rows, :]
                return i["w_ada"][b // 3, rows, (b % 3) * 2048:(b % 3 + 1) * 2048]

            for t in range(2, 4):
                sp.dma_start(x_in[:, t, :], i["x_prompt"][0, t * P:(t + 1) * P, :]).then_inc(x_loaded[t], 16)
            sp.dma_start(x_in[0:NS, 4, :], i["x_sample"][0, :, :]).then_inc(x_loaded[4], 16)
            for dup in range(2):
                sp.dma_start(kc_in[:, 0, :, dup, :], i["cache_a_k"][0, 0, 0:P]).then_inc(cache_in, 16)
                sp.dma_start(kc_in[:, 1, :, dup, :], i["cache_a_k"][0, 0, P:2 * P]).then_inc(cache_in, 16)
                sp.dma_start(kic_in[:, :, dup, :],
                             i["cache_a_kidx"][0, 0].rearrange("(t p) d -> p t d", p=P)).then_inc(cache_in, 16)
            for kt in range(KT):
                if kt >= 6:
                    sp.wait_ge(ada_used, kt - 5)
                sp.dma_start(ada0_slot(kt), ada_src(0, kt)).then_inc(ada0_in[kt], 16)

            def w_load(u, src, kt, cols, it=0, per=0):
                if u >= 2:
                    sp.wait_ge(wlo_done, per * it + u - 1)
                sp.dma_start(w_raw[:, u % 2, 0:kt * cols].rearrange("p (t n) -> p t n", t=kt),
                             src.rearrange("(t p) n -> p t n", p=P)).then_inc(raw_in[u % 2], 16)

            wa = i["w_in_a"][0]
            w_load(U_KIW, wa[:, 2048:2120], KT, 72)
            for j in range(4):
                w_load(U_QI + j, wa[:, 1536 + j * P:1536 + (j + 1) * P], KT, P)
                if j == 0:
                    sp.wait_ge(t_free, T_KIC + 1)
                    sp.wait_ge(rstd_spread, 1)
                    sp.wait_ge(ada_used, KT)
                    sp.dma_start(tables[:, :, :], i["consts"][:, NCONST:].rearrange("p (k t) -> p k t", k=4))\
                      .then_inc(const_in, 16)
                    sp.dma_start(v4[:, 4:6, :], i["cache_a_v"][0, 0].rearrange("(t p) g d -> p t (g d)", p=P))\
                      .then_inc(cache_in, 16)
            for j in range(2):
                w_load(U_K + j, wa[:, 1024 + j * P:1024 + (j + 1) * P], KT, P)
            for j in range(2):
                w_load(U_V + j, wa[:, 1280 + j * P:1280 + (j + 1) * P], KT, P)
            w_load(U_Q, wa[:, 0:P], KT, P)
            for n in range(KT, KT + 2):
                ada_load(n, ada_src(1, n - KT))
            for j in range(1, 3):
                w_load(U_Q + j, wa[:, j * P:(j + 1) * P], KT, P)
            for j in range(3, PAIRS):
                w_load(U_Q + j, wa[:, j * P:(j + 1) * P], KT, P)
                for n in range(2 * j + 4, 2 * j + 6):
                    ada_load(n, ada_src(n // KT, n % KT))

            def out_loads(u0, w, kt, done=0):
                with sp.Fori(0, KT // 2 - done) as it:
                    for r in range(2):
                        w_load(u0 + 2 * done + r, w[:, ds((2 * it + 2 * done + r) * P, P)], kt, P, it, 2)

            def ffn_half_loads(layer, half, u0):
                wi, wo = i["w_ffn_in"][layer], i["w_ffn_out"][layer]
                t0 = half * HT

                def tile(u, t, it, per):
                    w_load(u, wi[:, ds(t * P, P)], KT, P, it, per)
                    w_load(u + 1, wi[:, ds(t * P + DFF, P)], KT, P, it, per)

                with sp.Fori(0, HT) as it:
                    tile(u0, it + t0, it, 2)
                out_loads(u0 + 2 * HT, wo[half * WCOL:(half + 1) * WCOL, :], HT)

            for m in range(2):
                w_load(U_OA + m, i["w_out_a"][0][:, m * P:(m + 1) * P], KT, P)
                for n in range(2 * (PAIRS + m) + 4, 2 * (PAIRS + m) + 6):
                    ada_load(n, ada_src(n // KT, n % KT))

            def ada_loads(src, it):
                for j in range(KT):
                    sp.wait_ge(ada_used, KT * it + 3 * KT + (j - 2 if j >= 3 else min(j - 1, 0)))
                    sp.dma_start(ada_place(j)[0], src[j * P:(j + 1) * P, :]).then_inc(ada_in[j % 3], 16)

            sp.wait_ge(sc_step, 33)
            with sp.Fori(0, 3) as it:
                ada_loads(i["w_ada"][1, :, ds(2048 * it, 2048)], it)
            ada_loads(i["w_ada_final"], 3)
            out_loads(U_OA, i["w_out_a"][0], KT, 1)
            ffn_half_loads(0, 0, U_F0)
            ffn_half_loads(0, 1, U_F0 + FFN_N)

            wb = i["w_in_b"][0]
            w_load(U_FG, wb[:, 4096:4112], KT, 16)
            w_load(U_B, wb[:, 0:P], KT, P)
            sp.wait_ge(act_ready, ACT_N2 + KT)
            sp.dma_start(lfc[:, :, :], i["cache_b_logf"][0, 0].rearrange("(t p) h -> p t h", p=P)).then_inc(lfc_in, 16)

            def kv_cache_load(par, pair, it=0, guard=True):
                if guard:
                    sp.wait_ge(pv_done, 8 * it + guard)
                cols = ds(pair * P, P)
                sp.dma_start(kc_b[:, par, :, :],
                             i["cache_b_k"][0, 0].rearrange("(t p) h d -> p t (h d)", p=P)[:, :, cols])\
                  .then_inc(kvc_in[par], 16)
                sp.dma_start(vS_b[:, par, 4:6, :],
                             i["cache_b_v"][0, 0].rearrange("(t p) h d -> p t (h d)", p=P)[:, :, cols])\
                  .then_inc(kvc_in[par], 16)

            def bias_load(par, pair, it=0, guard=True):
                if guard:
                    sp.wait_ge(max_done, 8 * it + guard)
                for e in range(2):
                    sp.dma_start(bk[:, par, e, :], cum_dram[ds(pair * 2 + e, 1), :].partition_broadcast(P))\
                      .then_inc(bk_in[par], 16)

            kv_cache_load(0, 0, guard=False)
            for c in range(1, 4):
                w_load(U_B + c, wb[:, c * D:c * D + P], KT, P)
            w_load(U_B + 4, wb[:, P:2 * P], KT, P)
            sp.wait_ge(lf_dve, LF_CUM)
            sp.dma_start(cum_dram, cum[:, :]).then_inc(cum_out, 16)
            sp.wait_ge(cum_out, 16)
            bias_load(0, 0, guard=False)
            bias_load(1, 1, guard=False)
            kv_cache_load(1, 1, guard=False)
            for c in range(1, 4):
                w_load(U_B + 4 + c, wb[:, c * D + P:c * D + 2 * P], KT, P)
            with sp.Fori(0, PAIRS // 2 - 1) as it:
                for r in range(2):
                    pair = 2 * it + r + 2
                    for c in range(4):
                        w_load(U_B + 8 + 4 * r + c, wb[:, ds(pair * P + c * D, P)], KT, P, it, 8)
                        if c == 1:
                            bias_load(r, pair, it, 4 * (PAIRS + r) + 4)
                            kv_cache_load(r, pair, it, 4 * (PAIRS + r) + 4)
            out_loads(U_OB, i["w_out_b"][0], KT)
            ffn_half_loads(1, 0, U_F1)
            ffn_half_loads(1, 1, U_F1 + FFN_N)

            for j in range(10):
                h, t = j // 5, j % 5
                sp.wait_ge(y_free[j % 2], j // 2 + 1)
                dst = o["y_p"][0, t * P:(t + 1) * P, :] if t < 4 else o["y_s"][0]
                sp.dma_start(dst[:, h * 512:(h + 1) * 512], y_tok[0:P if t < 4 else NS, j, :]).then_inc(y_sent, 16)
            sp.wait_ge(out_sent, 16 * N_OUT_A)
            sp.wait_ge(kv_sent, 16 * 4 * PAIRS)
            sp.wait_ge(y_sent, 16 * 10)

        @block.tensor
        def _(pe):
            def lin_part(u, part, kt, m, hi, lo, it=0, per=0, ready=None):
                steps = [(p, t) for p in range(3) for t in range(kt)]
                if part is not None:
                    a, b = ((0, 6), (6, 9), (9, 12), (0, 4), (4, 8), (8, 12))[part]
                    steps = steps[a * kt // 4:b * kt // 4]
                if steps[0] == (0, 0):
                    pe.wait_ge(whi_done, per * it + u + 1)
                    if u >= 2:
                        pe.wait_ge(lin_free[u % 2], (per // 2) * it + u // 2)
                for p, t in steps:
                    if (p, t) == (1, 0):
                        pe.wait_ge(wlo_done, per * it + u + 1)
                    if ready is not None and p != 1:
                        have, base = ready[p // 2]
                        pe.wait_ge(have, base + t + 1)
                    w = (w_lo if p == 1 else w_hi)[:, u % 2, t * m:(t + 1) * m]
                    for h in range(2):
                        tok = slice(h * HALF, (h + 1) * HALF)
                        last = nc.tensor.matmul(lin[0:m, u % 2, h, 0:HALF], w, (lo if p == 2 else hi)[:, t, tok],
                                                start=(p == 0 and t == 0), stop=(p == 2 and t == kt - 1))
                if steps[-1] == (2, kt - 1):
                    last.then_inc(mm_done, 1)

            def after_norm(u, m, base):
                for p, v, cols in ((0, u, m), (1, u, m), (0, u + 1, P), (1, u + 1, P), (2, u, m), (2, u + 1, P)):
                    lin_part(v, 3 + p, KT, cols, act_hi, act_lo, ready=split_ready(base) if v == u else None)

            def split_ready(base):
                return (acthi_done, base), (act_ready, base)

            def linear(u, kt=KT, m=P, it=0, per=0, ready=None, hi=act_hi, lo=act_lo):
                lin_part(u, None, kt, m, hi, lo, it, per, ready)

            def t_use(n, it=0, per=0):
                if n >= 1:
                    pe.wait_ge(t_free, per * it + n)

            def ada_step(n, first=False):
                b, kt = n // KT, n % KT
                if b == 0:
                    pe.wait_ge(ada0_in[kt], 16)
                else:
                    pe.wait_ge(ada_in[n % 2], 16 * ((n - KT) // 2 + 1))
                if kt == 0 and b >= 1:
                    pe.wait_ge(ada_row_done, b)
                for j in range(4):
                    last = nc.tensor.matmul(O[32 * j:32 * j + 32, 0:512], cs_w[:, kt, :],
                                            (ada0_slot(kt) if b == 0 else ada_raw[:, n % 2, :])[:, 512 * j:512 * j + 512],
                                            start=(kt == 0), stop=(kt == KT - 1))
                last.then_inc(ada_used, 1)

            def ada_transpose(b, t):
                pe.wait_ge(ada_row_done, b + 1)
                t_use(t)
                for c in range(4):
                    last = nc.tensor.transpose(T[:, c * P:(c + 1) * P], ada_row[:, c * P:(c + 1) * P], ident)
                last.then_inc(t_ready, 1)

            pe.wait_ge(const_in, 16)
            pe.wait_ge(rows_in, 16 * 8)
            nc.tensor.transpose(T[:, 0:P], rows1[:, :], ident).then_inc(t_ready, 1)
            t_use(1)
            nc.tensor.transpose(T[:, 0:40], rows2[:, :], ident[0:40, 0:40]).then_inc(t_ready, 1)
            for t in range(5):
                pe.wait_ge(x_loaded[t], 16)
                w = P if t < 4 else NS
                for h in range(2):
                    t_use(T_X + 2 * t + h)
                    for j in range(4):
                        c = (4 * h + j) * P
                        last = nc.tensor.transpose(T[:, j * P:j * P + w], x_in[0:w, t, c:c + P], ident[0:w, 0:w])
                    last.then_inc(t_ready, 1)
            pe.wait_ge(cache_in, 16 * 6)
            for h in range(2):
                t_use(T_KC + h)
                for g in range(2):
                    for t in range(2):
                        last = nc.tensor.transpose(T[:, (2 * g + t) * P:(2 * g + t + 1) * P],
                                                   kc_in[:, t, 2 * h + g, :, :], ident)
                last.then_inc(t_ready, 1)
            t_use(T_KIC)
            for t in range(2):
                last = nc.tensor.transpose(T[:, t * P:(t + 1) * P], kic_in[:, t, :, :], ident)
            last.then_inc(t_ready, 1)
            def norm_sums(nz):
                if nz == 0:
                    pe.wait_ge(ones_done, 1)
                pe.wait_ge(ssq_done, KT * (nz + 1))
                pe.wait_ge(sq_done, KT * (nz + 1))
                for t in range(5):
                    tok = slice(t * P, (t + 1) * P) if t < 4 else slice(TOK - P, TOK)
                    nc.tensor.matmul(S[:, 0, t:t + 1], ssq[:, tok], ones[:, 0:1], start=True, stop=False)
                    last = nc.tensor.matmul(S[:, 0, t:t + 1], sq[:, (KT - 1) % 2, tok], ones[:, 0:1],
                                            start=False, stop=True)
                last.then_inc(ss_done, 1)
                pe.wait_ge(rstd_done, nz + 1)
                for t in range(5):
                    out = S[:, 1, t * P:(t + 1) * P] if t < 4 else S[:, 0, P:2 * P]
                    last = nc.tensor.transpose(out, rstd[:, t:t + 1].broadcast_to([P, P]), ident)
                last.then_inc(rstd_spread, 1)

            pe.wait_ge(cs_done, 1)
            for kt in range(6):
                ada_step(kt)
            norm_sums(0)
            for kt in range(6, KT):
                ada_step(kt)
            ada_transpose(0, T_ADA0)

            def rope_perm(u):
                r = rope_of(u)
                pe.wait_ge(raw_done, r + 1)
                rows, pm = (64, perm_i[0:64, 0:64]) if u == U_KIW else (P, perm_i if u < U_K else perm_q)
                for h in range(2):
                    last = nc.tensor.matmul(lin[0:rows, u % 2, h, 0:HALF], pm,
                                            rawb[0:rows, r % 2, h * HALF:(h + 1) * HALF], start=True, stop=True)
                last.then_inc(perm_done, 1)

            def token_major(src, t0):
                for e in range(2):
                    t_use(t0 + e)
                    for t in (range(4) if e == 0 else (4,)):
                        w = P if t < 4 else NS
                        last = nc.tensor.transpose(T[0:w, (t % 4) * P:(t % 4 + 1) * P],
                                                   src[:, t * P:t * P + w], ident)
                    last.then_inc(t_ready, 1)

            after_norm(U_KIW, 72, ACT_N0)
            rope_perm(U_KIW)
            linear(U_QI + 1)
            rope_perm(U_QI)
            linear(U_QI + 2)
            rope_perm(U_QI + 1)
            pe.wait_ge(rope_done, 1)
            t_use(T_KIW)
            for t in range(5):
                w = P if t < 4 else NS
                kcol = t * P if t < 4 else NP_ + PAST
                nc.tensor.transpose(T[0:w, t * 72:t * 72 + 64], kiT[0:64, kcol:kcol + w], ident[0:64, 0:64])
                last = nc.tensor.transpose(T[0:w, t * 72 + 64:t * 72 + 72], vTb[64:72, t * P:t * P + w],
                                           ident[64:72, 64:72])
            last.then_inc(t_ready, 1)
            linear(U_QI + 3)
            rope_perm(U_QI + 2)
            linear(U_K)
            rope_perm(U_QI + 3)

            def idx_unit(n):
                qt, j = 3 - n // 4, n % 4
                if n == 0:
                    pe.wait_ge(rope_done, 5)
                    pe.wait_ge(kidup_done, 1)
                if n >= 1:
                    pe.wait_ge(rel_done, n)
                rows, tok, keys, nk = ((P, qt * P, 0, (qt + 1) * P) if qt else (NS, NP_, NP_, PAST + NS))
                for e in range(2):
                    r = slice(64 * e, 64 * e + 64)
                    last = nc.tensor.matmul(S[0:rows, e, 0:nk], qiT[r, j, tok:tok + rows], kiT[r, keys:keys + nk],
                                            start=True, stop=True)
                last.then_inc(idx_done, 1)

            for j, u in enumerate((U_K + 1, U_V, U_V + 1, U_Q)):
                idx_unit(4 * j)
                lin_part(u, 0, KT, P, act_hi, act_lo)
                idx_unit(4 * j + 1)
                lin_part(u, 1, KT, P, act_hi, act_lo)
                idx_unit(4 * j + 2)
                lin_part(u, 2, KT, P, act_hi, act_lo)
                idx_unit(4 * j + 3)
                if j == 0:
                    rope_perm(U_K)
                if j == 1:
                    rope_perm(U_K + 1)
                    pe.wait_ge(rope_done, rope_of(U_K) + 1)
                    token_major(kR, T_K0)
                if j == 2:
                    pe.wait_ge(rope_done, rope_of(U_K + 1) + 1)
                    token_major(kR, T_K0 + 2)
                    pe.wait_ge(lin_free[U_V % 2], free_count(U_V))
                    token_major(vTb, T_V0)
                if j == 3:
                    pe.wait_ge(lin_free[(U_V + 1) % 2], free_count(U_V + 1))
                    token_major(vTb, T_V0 + 2)
            ada_step(KT)
            ada_step(KT + 1)
            for j in range(1, PAIRS):
                linear(U_Q + j)
                rope_perm(U_Q + j - 1)
                for n in range(KT + 2 * j, KT + 2 * j + 2):
                    ada_step(n)
                if j == 4:
                    ada_transpose(1, T_ADA1)
            rope_perm(U_Q + PAIRS - 1)

            def s_unit(k, par, n, it, per, qS, kS, ready, forget):
                for q, v in ready:
                    pe.wait_ge(q, v)
                if n >= 1:
                    pe.wait_ge(max_done, per * it + n)
                groups = [(0, P, k * P, 0, (k + 1) * P, 384 if k == 0 else 0)]
                if k == 0:
                    groups.append((1, NS, NP_, NP_, PAST + NS, 0))
                for sample, rows, tok, key, nk, col in groups:
                    for e in range(2):
                        r = slice(64 * e, 64 * e + 64)
                        out = S[64 * e:64 * e + 64] if sample else S[0:P]
                        last = nc.tensor.matmul(out[:, e, col:col + nk], qS[r, tok:tok + rows],
                                                kS[r, key:key + nk], start=True, stop=not forget)
                    if forget:
                        for e in range(2):
                            r = slice(64 * e, 64 * e + 64)
                            c = col + nk - rows
                            if sample:
                                last = nc.tensor.matmul(S[r, e, c:c + rows], ident_b[r, r], tri_b[r, r],
                                                        start=False, stop=True)
                            else:
                                last = nc.tensor.matmul(S[:, e, c:c + rows], ident_b[:, :], tri_b[:, :],
                                                        start=False, stop=True)
                last.then_inc(s_done, 1)

            def t_unit(k, use, par, n, t, it, per, tper, pr, ps):
                if use == 0:
                    pe.wait_ge(norm_done, per * it + n + 1)
                t_use(t, it, tper)
                if k == 0 and use == 0:
                    for e in range(2):
                        last = nc.tensor.transpose(T[:, e * P:(e + 1) * P], probs(pr, 0, e), ident)
                elif k == 0:
                    for b in range(3):
                        w = P if b < 2 else NS
                        last = nc.tensor.transpose(T[0:w, b * P:(b + 1) * P], ps[:, b * P:b * P + w], ident)
                else:
                    for b in range(k + 1):
                        last = nc.tensor.transpose(T[:, b * P:(b + 1) * P], probs(pr, k, use)[:, b * P:(b + 1) * P], ident)
                last.then_inc(t_ready, 1)

            def pv_unit(k, n, pair, t, it, per, tper, pT, pTs, vS, split, so_col=0):
                pe.wait_ge(t_free, tper * it + t + 1)
                if k == 0 and pair >= 1:
                    pe.wait_ge(o_free, (per // 4) * it + pair)
                if k == 0:
                    for b in range(3):
                        w = P if b < 2 else NS
                        for e in range(2):
                            v = vS[0:w, 4 + b, 64 * e:64 * e + 64] if split else vS[0:w, 4 + b, :]
                            last = nc.tensor.matmul(T[64 * e:64 * e + 64, so_col:so_col + NS], v, pTs[0:w, b, 64 * e:64 * e + 64],
                                                    start=(b == 0), stop=(b == 2))
                    last.then_inc(so_ready if so_col else t_ready, 1)
                for b in range(k + 1):
                    for e in range(2):
                        v = vS[:, b, 64 * e:64 * e + 64] if split else vS[:, b, :]
                        last = nc.tensor.matmul(O[64 * e:64 * e + 64, k * P:(k + 1) * P], v,
                                                pT[:, e, b * P:(b + 1) * P], start=(b == 0), stop=(b == k))
                last.then_inc(pv_done, 1)

            def s_wait(n, it):
                if n >= 2:
                    pe.wait_ge(max_done, 8 * it + n - 1)
                if n % 4 == 0:
                    pe.wait_ge(q_staged, 2 * it + n // 4 + 1)
                if n % 8 == 0:
                    pe.wait_ge(k_staged, it + n // 8 + 1)

            def sa_unit(n, it):
                k, par, bank = n % 4, (n // 4) % 2, (S, S2)[n % 2]
                groups = [(0, P, k * P, 0, (k + 1) * P, 384 if k == 0 else 0)]
                if k == 0:
                    groups.append((1, NS, NP_, NP_, PAST + NS, 0))
                for sample, rows, tok, key, nk, col in groups:
                    for e in range(2):
                        r = slice(64 * e, 64 * e + 64)
                        out = bank[64 * e:64 * e + 64] if sample else bank[0:P]
                        last = nc.tensor.matmul(out[:, e, col:col + nk], qS_a[r, par, tok:tok + rows],
                                                kS_a[r, key:key + nk],
                                                start=True, stop=True)
                last.then_inc(s_done, 1)

            def ta_unit(n, t, it):
                k = n % 4
                pe.wait_ge(norm_done, 8 * it + n + 1)
                if k == 1:
                    pe.wait_ge(so_free, 2 * it + n // 4 + 1)
                t_use(t, it, 9)
                for b in range(max(k + 1, 2)):
                    src = probs(pr_a, 0, b) if k == 0 else probs(pr_a, k, 0)[:, b * P:(b + 1) * P]
                    last = nc.tensor.transpose(T[:, b * P:(b + 1) * P], src, ident)
                last.then_inc(t_ready, 1)
                if n >= 1:
                    pe.wait_ge(t2_free, 8 * it + n)
                for b in range(3 if k == 0 else k + 1):
                    src = ps_a[:, b * P:min((b + 1) * P, PAST + NS)] if k == 0 else probs(pr_a, k, 1)[:, b * P:(b + 1) * P]
                    w = NS if k == 0 and b == 2 else P
                    last = nc.tensor.transpose(T2[0:w, b * P:(b + 1) * P], src, ident)
                last.then_inc(t2_ready, 1)

            def ada_chunk(j, it):
                place, per_batch = ada_place(j)
                pe.wait_ge(ada_in[j % 3], 16 * per_batch * it + 16 * ((0 if j % 3 == 2 else 8) + j // 3 + 1))
                if j == 0:
                    pe.wait_ge(ada_row_done, it + 3)
                for c in range(4):
                    last = nc.tensor.matmul(adaO[32 * c:32 * c + 32, 0:512], cs_w[:, j, :],
                                            place[:, 512 * c:512 * c + 512],
                                            start=(j == 0), stop=(j == KT - 1))
                last.then_inc(ada_used, 1)

            def a_body(it, last_turn):
                for n in range(8):
                    k, r = n % 4, n // 4
                    t = T_A + n
                    more = not (last_turn and n >= 6)
                    if more:
                        s_wait(n + 2, it)
                    ta_unit(n, t, it)
                    if more:
                        sa_unit(n + 2, it)
                    for j in ((n,) if n < 6 else (6, 7) if n == 6 else ()):
                        ada_chunk(j, it)
                    if n == 0:
                        pe.wait_ge(v_staged, it + 1)
                    pe.wait_ge(t2_free, 8 * it + n + 1)
                    pv_unit(k, n, r, t, it, 8, 9, pT_a, pTs_a, vS_a, False, 2 * P)
                pe.wait_ge(ada_row_done, it + 4)
                t_use(T_A + 8, it, 9)
                for c in range(4):
                    last = nc.tensor.transpose(T[:, c * P:(c + 1) * P], ada_row[:, c * P:(c + 1) * P], ident)
                last.then_inc(t_ready, 1)

            pe.wait_ge(lin_free[(U_OA - 1) % 2], free_count(U_OA - 1))
            pe.wait_ge(lin_free[(U_OA - 2) % 2], free_count(U_OA - 2))
            for n in range(2):
                s_wait(n, 0)
                sa_unit(n, 0)
            ada_transpose(2, T_ADA2)
            with pe.Fori(0, PAIRS // 2 - 1) as it:
                a_body(it, False)
            a_body(PAIRS // 2 - 1, True)
            pe.wait_ge(t2_free, 4 * PAIRS)
            pe.wait_ge(t_free, T_ADA[6])

            def out_linear(u0, kt, ready, hi, lo):
                for r in range(2):
                    linear(u0 + r, kt, ready=ready if r == 0 else None, hi=hi, lo=lo)
                with pe.Fori(0, KT // 2 - 1) as it:
                    for r in range(2):
                        linear(u0 + 2 + r, kt, P, it, 2, None, hi, lo)

            def ffn_half(u0, act_base, hid_base):
                done = 0
                if act_base is not None:
                    after_norm(u0, P, act_base)
                    done = 1
                with pe.Fori(0, HT - done) as it:
                    for g in range(2):
                        linear(u0 + 2 * done + g, it=it, per=2)
                out_linear(u0 + 2 * HT, HT, ((hid_ready, hid_base),) * 2, hid_hi, hid_lo)

            out_linear(U_OA, KT, ((ohi_done, 0), (olo_done, 0)), act_hi, act_lo)
            norm_sums(1)
            ffn_half(U_F0, ACT_N1, 0)
            ffn_half(U_F0 + FFN_N, None, HT)
            norm_sums(2)

            after_norm(U_FG, 16, ACT_N2)
            pe.wait_ge(lfc_in, 16)
            t_use(T_LF)
            for t in range(2):
                last = nc.tensor.transpose(T[0:16, t * P:(t + 1) * P], lfc[:, t, :], ident)
            last.then_inc(t_ready, 1)

            def k_tokens(half, par, kp, t, it=0, tper=0, per=0):
                t_use(t + half, it, tper)
                if half == 0:
                    pe.wait_ge(lin_free[kp % 2], (per // 2) * it + free_count(kp))
                    for c in range(4):
                        last = nc.tensor.transpose(T[:, c * P:(c + 1) * P], kS_b[:, par, c * P:(c + 1) * P], ident)
                    last.then_inc(t_ready, 1)
                    return
                pe.wait_ge(kvc_in[par], 16 * 2 * (per // 8) * it + 32 * KVC_ROUND[kp])
                for c in range(2):
                    nc.tensor.transpose(T[:, (c + 1) * P:(c + 2) * P], kc_b[:, par, c, :], ident)
                nc.tensor.transpose(T[0:NS, 0:P], kS_b[:, par, NP_ + PAST:NK], ident).then_inc(t_ready, 1)

            def v_tokens(half, vp, t, it=0, tper=0, per=0):
                if half == 0:
                    pe.wait_ge(lin_free[vp % 2], (per // 2) * it + free_count(vp))
                t_use(t + half, it, tper)
                for c in (range(3) if half == 0 else (3, 4)):
                    w = P if c < 4 else NS
                    last = nc.tensor.transpose(T[0:w, (c % 3) * P:(c % 3 + 1) * P],
                                               vTb_b[:, c * P:c * P + w], ident)
                last.then_inc(t_ready, 1)

            linear(U_B + 1)
            linear(U_B + 2)
            k_tokens(0, 0, U_B + 1, T_B0)
            k_tokens(1, 0, U_B + 1, T_B0)
            pe.wait_ge(lf_dve, LF_DONE)
            t_use(T_LFO)
            for t in range(5):
                w = P if t < 4 else NS
                last = nc.tensor.transpose(T[0:w, t * 16:(t + 1) * 16], lb[:, t * P:t * P + w], ident[0:16, 0:16])
            last.then_inc(t_ready, 1)
            s_unit(0, 0, 32, 0, 8, qS_b[:, 0, :], kS_b[:, 0, :],
                   [(lin_free[U_B % 2], free_count(U_B)), (t_free, T_B0 + 2)], True)
            linear(U_B + 3)
            v_tokens(0, U_B + 2, T_B0 + 3)
            v_tokens(1, U_B + 2, T_B0 + 3)

            def b_ready(u, par, rnd, it, per):
                return [(lin_free[u % 2], (per // 2) * it + free_count(u)),
                        (lin_free[(u + 1) % 2], (per // 2) * it + free_count(u + 1)),
                        (bk_in[par], 32 * it * (per > 0) + 32 * rnd)]

            def b_body(it, last_turn):
                for r in range(2):
                    nxt = not (last_turn and r == 1)
                    for k in range(4):
                        n = 32 + 4 * r + k
                        u = U_B + 4 * (r + 1) + k
                        t = T_B + 13 * r + (0, 3, 5, 9)[k]
                        if not nxt:
                            t = T_B + 13 * r + (0 if k == 0 else 1 + 2 * k)
                        t_unit(k, 0, r, n, t, it, 8, 26, pr_b, ps_b)
                        if not (last_turn and r == 1 and k == 3):
                            k2, r2 = (k + 1) % 4, r + (k == 3)
                            ready = []
                            if k2 == 0:
                                ready = b_ready(U_B + 4 * r2, r2 % 2, 1 + r2 // 2, it, 8)
                                ready.append((t_free, 26 * it + T_B + 13 * r + 9))
                            s_unit(k2, r2 % 2, n + 1, it, 8, qS_b[:, r2 % 2, :], kS_b[:, r2 % 2, :], ready, True)
                        t_unit(k, 1, r, n, t + 1, it, 8, 26, pr_b, ps_b)
                        if nxt:
                            lin_part(u, 0, KT, P, act_hi, act_lo, it, 8)
                        pv_unit(k, n, PAIRS + r, t + 1, it, 8, 26, pT_b, pTs_b, vS_b[:, r, :, :], True)
                        for half in range(2 if nxt else 0):
                            if k == 2:
                                k_tokens(half, (r + 1) % 2, u - 1, T_B + 13 * r + 7, it, 26, 8)
                            if k == 3:
                                v_tokens(half, u - 1, T_B + 13 * r + 11, it, 26, 8)
                            lin_part(u, 1 + half, KT, P, act_hi, act_lo, it, 8)

            with pe.Fori(0, PAIRS // 2 - 1) as it:
                b_body(it, False)
            b_body(PAIRS // 2 - 1, True)

            out_linear(U_OB, KT, split_ready(ACT_OB), act_hi, act_lo)
            norm_sums(3)
            ffn_half(U_F1, ACT_N3, 2 * HT)
            ffn_half(U_F1 + FFN_N, None, 3 * HT)
            norm_sums(4)
            for j in range(10):
                h, t = j // 5, j % 5
                w = P if t < 4 else NS
                pe.wait_ge(f_done, 4 * h + 4)
                if j >= 6:
                    pe.wait_ge(y_free[j % 2], (j - 6) // 2 + 1)
                for c in range(4):
                    last = nc.tensor.transpose(y_bank[j % 6][0:w, c * P:(c + 1) * P], fo[:, 4 * h + c, t * P:t * P + w], ident)
                last.then_inc(y_ready, 1)

        @block.scalar
        def _(act):
            A = nc.scalar.activation

            def split_hi(u, n, it=0, per=0):
                act.wait_ge(raw_in[u % 2], 16 * ((per // 2) * it + u // 2 + 1))
                if u >= 2:
                    act.wait_ge(mm_done, per * it + u - 1)
                A(w_hi[:, u % 2, 0:n], w_raw[:, u % 2, 0:n], ACT.Copy).then_inc(whi_done, 1)

            def halves(dst):
                return dst.rearrange("p (h t) -> p h t", h=2)

            act.wait_ge(cs_zero, 1)
            act.wait_ge(t_free, 1)
            A(cs_w[:, :, 0:2], vecs[:, 112:128].rearrange("p (s k) -> p k s", s=2), ACT.Silu).then_inc(cs_done, 1)

            def square(nz, m, it=0, per=0):
                if m >= 2 or per:
                    act.wait_ge(ssq_done, per * it + KT * nz + m)
                if nz >= 1 and m < 2:
                    act.wait_ge(ss_done, nz)
                A(sq[:, m % 2, :], x[:, ds(per * it + m, 1), :].rearrange("p a c -> p (a c)"), ACT.Square)\
                    .then_inc(sq_done, 1)

            def norm(nz, act_base, between=None):
                A(root[:, 5:6], eps[:, 0:1], ACT.Sqrt)
                act.wait_ge(ss_done, nz + 1)
                A(root[:, 0:5], S[:, 0, 0:5], ACT.Sqrt, scale=1.0 / D, bias=eps[:, 0:1]).then_inc(root_done, 1)
                if between is not None:
                    between()
                for kt in range(KT):
                    act.wait_ge(y_done, KT * nz + kt + 1)
                    dst = act_hi if act_base is not None else fo
                    for c0, c1, st in ((0, NP_, 0), (NP_, TOK, 1)):
                        last = A(dst[:, kt, c0:c1], fo[:, kt, c0:c1], ACT.Identity, bias=mods[:, SHIFT[nz] + kt, st:st + 1])
                    last.then_inc(acthi_done if act_base is not None else f_done, 1)

            def ada_evac(b):
                act.wait_ge(ada_used, KT * (b + 1))
                if b >= 1:
                    act.wait_ge(t_ready, T_ADA[b - 1] + 1)
                A(ada_row[:, :], O[:, :], ACT.Copy).then_inc(ada_row_done, 1)

            act.wait_ge(ones_done, 2)

            act.wait_ge(t_free, T_KC)
            for kt in range(KT):
                square(0, kt)
            norm(0, ACT_N0, lambda: (ada_evac(0), split_hi(U_KIW, KT * 72)))

            def raw_evac(u):
                r = rope_of(u)
                act.wait_ge(mm_done, u + 1)
                if r >= 2:
                    act.wait_ge(rope_done, r - 1)
                rows = 64 if u == U_KIW else P
                A(halves(rawb[0:rows, r % 2, :]), lin[0:rows, u % 2, :, 0:HALF], ACT.Copy).then_inc(raw_done, 1)

            def perm_evac(u):
                r = rope_of(u)
                act.wait_ge(perm_done, r + 1)
                rows = 64 if u == U_KIW else P
                A(halves(permb[0:rows, r % 2, :]), lin[0:rows, u % 2, :, 0:HALF], ACT.Copy)\
                    .then_inc(lin_free[u % 2], 1)

            def v_evac(u):
                act.wait_ge(mm_done, u + 1)
                if u == U_V:
                    act.wait_ge(t_ready, T_KIW + 1)
                else:
                    act.wait_ge(t_ready, T_V0 + 2)
                A(halves(vTb[:, :]), lin[:, u % 2, :, 0:HALF], ACT.Copy).then_inc(lin_free[u % 2], 1)

            def k_dup(j):
                act.wait_ge(rope_done, rope_of(U_K + j) + 1)
                for e in range(2):
                    for half in range(2):
                        for c0, c1, d0 in ((0, NP_, 0), (NP_, TOK, NP_ + PAST)):
                            last = A(kT4[64 * half:64 * half + 64, 2 * j + e, d0:d0 + c1 - c0],
                                     kR[64 * e:64 * e + 64, c0:c1], ACT.Copy)
                last.then_inc(kdup_done, 1)

            def token_major_evac(dst, cols, t0):
                act.wait_ge(t_ready, t0 + 1)
                A(dst[:, 0:4, cols], T[:, :].rearrange("p (t c) -> p t c", t=4), ACT.Copy).then_inc(t_free, 1)
                row = 4 if dst is kout else 6
                act.wait_ge(t_ready, t0 + 2)
                A(dst[0:NS, row, cols], T[0:NS, 0:P], ACT.Copy).then_inc(t_free, 1)

            N = KT * P
            split_hi(U_QI, N)
            raw_evac(U_KIW)
            A(halves(vTb[64:72, :]), lin[64:72, 0, :, 0:HALF], ACT.Copy)
            perm_evac(U_KIW)
            split_hi(U_QI + 1, N)
            raw_evac(U_QI)
            split_hi(U_QI + 2, N)
            perm_evac(U_QI)
            raw_evac(U_QI + 1)
            act.wait_ge(rope_done, 1)
            A(kiT[64:P, 0:NP_], kiT[0:64, 0:NP_], ACT.Copy)
            A(kiT[64:P, NP_ + PAST:NK], kiT[0:64, NP_ + PAST:NK], ACT.Copy).then_inc(kidup_done, 1)
            split_hi(U_QI + 3, N)
            perm_evac(U_QI + 1)
            raw_evac(U_QI + 2)
            act.wait_ge(t_ready, T_KIW + 1)
            Tk = T[:, 0:360].rearrange("p (t c) -> p t c", t=5)
            A(kiout[:, 0:4, :], Tk[:, 0:4, 0:64], ACT.Copy)
            A(wi_t[:, 0:4, :], Tk[:, 0:4, 64:72], ACT.Copy, scale=(NIDX * HD) ** -0.5)
            A(kiout[0:NS, 4, :], Tk[0:NS, 4, 0:64], ACT.Copy)
            A(wi_t[0:NS, 4, :], Tk[0:NS, 4, 64:72], ACT.Copy, scale=(NIDX * HD) ** -0.5).then_inc(t_free, 1)
            act.wait_ge(t_free, T_KIW + 1)
            act.dma_start(o["kidx_p"][0, 0].rearrange("(t p) d -> p t d", p=P), kiout[:, 0:4, :]).then_inc(out_sent, 16)
            act.dma_start(o["kidx_s"][0, 0], kiout[0:NS, 4, :]).then_inc(out_sent, 16)
            split_hi(U_K, N)
            perm_evac(U_QI + 2)
            raw_evac(U_QI + 3)
            split_hi(U_K + 1, N)
            perm_evac(U_QI + 3)
            raw_evac(U_K)

            def idx_relu(n):
                qt = 3 - n // 4
                rows, nk = (P, (qt + 1) * P) if qt else (NS, PAST + NS)
                act.wait_ge(idx_done, n + 1)
                if n >= 1:
                    act.wait_ge(sc_step, 2 * n)
                A(rel[0:rows, :, 0:nk], S[0:rows, :, 0:nk], ACT.Relu).then_inc(rel_done, 1)

            nxt = {0: U_V, 1: U_V + 1, 2: U_Q, 3: U_Q + 1}
            for j in range(4):
                idx_relu(4 * j)
                split_hi(nxt[j], N)
                for e in range(1, 4):
                    idx_relu(4 * j + e)
                if j == 0:
                    perm_evac(U_K)
                    raw_evac(U_K + 1)
                if j == 1:
                    k_dup(0)
                    perm_evac(U_K + 1)
                    token_major_evac(kout, slice(0, P), T_K0)
                    v_evac(U_V)
                if j == 2:
                    k_dup(1)
                    token_major_evac(kout, slice(P, 2 * P), T_K0 + 2)
                    token_major_evac(v4, slice(0, P), T_V0)
                    v_evac(U_V + 1)
                if j == 3:
                    token_major_evac(v4, slice(P, 2 * P), T_V0 + 2)
            act.wait_ge(t_free, T_V0 + 4)
            for name, buf, row in (("a_k", kout, 4), ("a_v", v4, 6)):
                act.dma_start(o[name + "_p"][0, 0].rearrange("(t p) g d -> p t (g d)", p=P), buf[:, 0:4, :])\
                    .then_inc(out_sent, 16)
                act.dma_start(o[name + "_s"][0, 0].rearrange("p g d -> p (g d)"), buf[0:NS, row, :])\
                    .then_inc(out_sent, 16)
            raw_evac(U_Q)
            for j in range(1, PAIRS):
                if j + 1 < PAIRS:
                    split_hi(U_Q + j + 1, N)
                else:
                    split_hi(U_OA, N)
                perm_evac(U_Q + j - 1)
                raw_evac(U_Q + j)
                if j == 3:
                    ada_evac(1)
            perm_evac(U_Q + PAIRS - 1)
            ada_evac(2)

            def exp_unit(k, n, it, per, pr, ps):
                act.wait_ge(max_done, per * it + n + 1)
                for e in range(2):
                    buf = probs(pr, k, e)
                    last = A(buf, buf, ACT.Exp, scale=-1.0, bias=negmax[:, k, e:e + 1],
                             accum_out=rowsum[:, k, e:e + 1])
                if k == 0:
                    last = A(ps[:, :], ps[:, :], ACT.Exp, scale=-1.0, bias=negmax[:, 0, 2:3],
                             accum_out=rowsum[:, 0, 2:3])
                last.then_inc(exp_done, 1)

            def pT_evac(k, t, n, it, per, tper, pT):
                act.wait_ge(t_ready, tper * it + t + 1)
                if n >= 1:
                    act.wait_ge(pv_done, per * it + n)
                if k == 0:
                    A(pT[:, :, 0:P], T[:, 0:2 * P].rearrange("p (e c) -> p e c", e=2), ACT.Copy).then_inc(t_free, 1)
                else:
                    A(pT[:, 0, 0:(k + 1) * P], T[:, 0:(k + 1) * P], ACT.Copy).then_inc(t_free, 1)

            def a_body(it, last_turn):
                for n in range(8):
                    k, r = n % 4, n // 4
                    t = T_A + n
                    pair = ds(2 * it + r, 1)
                    pT_evac(k, t, n, it, 8, 9, pT_a)
                    if not (last_turn and n >= 6):
                        exp_unit((k + 2) % 4, n + 2, it, 8, pr_a, ps_a)
                    if k == 0:
                        act.wait_ge(so_ready, 2 * it + r + 1)
                        A(qo[:, pair, NP_:TOK], T[:, 2 * P:2 * P + NS].rearrange("p (a c) -> p a c", a=1), ACT.Copy)\
                            .then_inc(so_free, 1)
                    if k == 3:
                        act.wait_ge(pv_done, 8 * it + n + 1)
                        A(qo[:, pair, 0:NP_], O[:, :].rearrange("p (a c) -> p a c", a=1), ACT.Copy)\
                            .then_inc(o_free, 1)
                    if n == 6:
                        act.wait_ge(ada_used, KT * it + 4 * KT)
                        act.wait_ge(t_ready, 9 * it + T_A)
                        A(ada_row[:, :], adaO, ACT.Copy).then_inc(ada_row_done, 1)

            exp_unit(0, 0, 0, 8, pr_a, ps_a)
            exp_unit(1, 1, 0, 8, pr_a, ps_a)
            with act.Fori(0, PAIRS // 2 - 1) as it:
                a_body(it, False)
            a_body(PAIRS // 2 - 1, True)
            act.wait_ge(o_free, PAIRS)
            act.wait_ge(ohi_done, PAIRS - 1)
            A(act_hi[:, PAIRS - 1, :], qo[:, PAIRS - 1, :], ACT.Copy).then_inc(ohi_done, 1)

            def split_o(pairs_done, base):
                act.wait_ge(o_free, pairs_done)
                for kt in range(KT):
                    A(act_hi[:, kt, :], qo[:, kt, :], ACT.Copy).then_inc(acthi_done, 1)

            def out_stage(u0, n, n_next, nz=None):
                def tile(r, it, per, cols, more=True):
                    if more:
                        split_hi(u0 + r + 1, cols, it, per)
                    if nz is not None:
                        act.wait_ge(lin_free[(u0 + r) % 2], (per // 2) * it + free_count(u0 + r))
                        square(nz, r, it, per)

                with act.Fori(0, KT // 2 - 1) as it:
                    for r in range(2):
                        tile(r, it, 2, n)
                tile(KT - 2, 0, 0, n)
                tile(KT - 1, 0, 0, n_next, bool(n_next))

            def ffn_half(u0, hid_base, n_next, nz=None):
                def tile(j, u, it, per, n2=N):
                    split_hi(u + 1, N, it, per)
                    act.wait_ge(mm_done, per * it + u + 1)
                    if u != U_F0:
                        act.wait_ge(hid_ready, (per // 2) * it + hid_base + j)
                    A(halves(sg[:, :]), lin[:, u % 2, :, 0:HALF], ACT.Silu).then_inc(lin_free[u % 2], 1)
                    split_hi(u + 2, n2, it, per)
                    act.wait_ge(lin_free[(u + 1) % 2], (per // 2) * it + free_count(u + 1))
                    A(hid_hi[:, ds(it + j, 1), :], hf[:, :].rearrange("p (a c) -> p a c", a=1), ACT.Copy)\
                        .then_inc(hidhi_done, 1)

                tile(0, u0, 0, 0)
                with act.Fori(0, HT - 2) as it:
                    tile(1, u0 + 2, it, 2)
                tile(HT - 1, u0 + 2 * HT - 2, 0, 0, HT * P)
                out_stage(u0 + 2 * HT, HT * P, n_next, nz)

            act.wait_ge(out_sent, 16 * 6)
            out_stage(U_OA, N, N, 1)
            norm(1, ACT_N1)
            ffn_half(U_F0, 0, N)
            ffn_half(U_F0 + FFN_N, HT, KT * 16, 2)
            norm(2, ACT_N2)

            split_hi(U_B, N)
            act.wait_ge(mm_done, U_FG + 1)
            A(halves(zb[:, :]), lin[0:16, U_FG % 2, :, 0:HALF], ACT.Identity, bias=bias_f[:, 0:1])\
                .then_inc(lin_free[U_FG % 2], 1)
            act.wait_ge(lin_free[U_FG % 2], free_count(U_FG))
            A(eb[:, :], zb[:, :], ACT.Abs).then_inc(lf_act, 1)
            act.wait_ge(lf_act, 1)
            A(eb[:, :], eb[:, :], ACT.Exp, scale=-1.0).then_inc(lf_act, 1)
            act.wait_ge(lf_dve, 1)
            A(lb[:, :], ub[:, :], ACT.Ln).then_inc(lf_act, 1)

            def q_evac(par, u, it=0, per=0):
                act.wait_ge(mm_done, per * it + u + 1)
                A(halves(qS_b[:, par, :]), lin[:, u % 2, :, 0:HALF], ACT.Copy).then_inc(lin_free[u % 2], 1)

            def v_evac_b(u, it=0, per=0):
                act.wait_ge(mm_done, per * it + u + 1)
                A(halves(vTb_b[:, :]), lin[:, u % 2, :, 0:HALF], ACT.Copy).then_inc(lin_free[u % 2], 1)

            def g_evac(par, u, it=0, per=0):
                act.wait_ge(mm_done, per * it + u + 1)
                A(halves(gsig[:, par, :]), lin[:, u % 2, :, 0:HALF], ACT.Exp, scale=-1.0).then_inc(lin_free[u % 2], 1)

            def k_tokens_evac(par, pair, t, sent, it=0, tper=0):
                act.wait_ge(t_ready, tper * it + t + 1)
                if sent is not None:
                    act.wait_ge(kv_sent, sent)
                A(kout_b[:, 0:4, :], T[:, :].rearrange("p (t c) -> p t c", t=4), ACT.Copy).then_inc(t_free, 1)
                act.wait_ge(t_ready, tper * it + t + 2)
                A(kout_b[0:NS, 4, :], T[0:NS, 0:P], ACT.Copy)
                A(kS_b[:, par, NP_:NP_ + PAST], T[:, P:3 * P], ACT.Copy).then_inc(t_free, 1)
                act.wait_ge(t_free, tper * it + t + 2)
                cols = ds(pair * P, P)
                act.dma_start(o["b_k_p"][0, 0].rearrange("(t p) h d -> p t (h d)", p=P)[:, :, cols], kout_b[:, 0:4, :])\
                    .then_inc(kv_sent, 16)
                act.dma_start(o["b_k_s"][0, 0].rearrange("p h d -> p (h d)")[:, cols], kout_b[0:NS, 4, :])\
                    .then_inc(kv_sent, 16)

            def v_tokens_evac(par, pair, t, it=0, tper=0):
                act.wait_ge(t_ready, tper * it + t + 1)
                A(vS_b[:, par, 0:3, :], T[:, 0:3 * P].rearrange("p (t c) -> p t c", t=3), ACT.Copy).then_inc(t_free, 1)
                act.wait_ge(t_ready, tper * it + t + 2)
                A(vS_b[:, par, 3, :], T[:, 0:P], ACT.Copy)
                A(vS_b[0:NS, par, 6, :], T[0:NS, P:2 * P], ACT.Copy).then_inc(t_free, 1)
                act.wait_ge(t_free, tper * it + t + 2)
                cols = ds(pair * P, P)
                act.dma_start(o["b_v_p"][0, 0].rearrange("(t p) h d -> p t (h d)", p=P)[:, :, cols],
                              vS_b[:, par, 0:4, :]).then_inc(kv_sent, 16)
                act.dma_start(o["b_v_s"][0, 0].rearrange("p h d -> p (h d)")[:, cols], vS_b[0:NS, par, 6, :])\
                    .then_inc(kv_sent, 16)

            split_hi(U_B + 1, N)
            q_evac(0, U_B)
            split_hi(U_B + 2, N)
            act.wait_ge(mm_done, U_B + 2)
            A(kS_b[:, 0, 0:HALF], lin[:, (U_B + 1) % 2, 0, 0:HALF], ACT.Copy)
            A(kS_b[:, 0, HALF:NP_], lin[:, (U_B + 1) % 2, 1, 0:NP_ - HALF], ACT.Copy)
            A(kS_b[:, 0, NP_ + PAST:NK], lin[:, (U_B + 1) % 2, 1, NP_ - HALF:HALF], ACT.Copy)\
                .then_inc(lin_free[(U_B + 1) % 2], 1)
            split_hi(U_B + 3, N)
            v_evac_b(U_B + 2)
            k_tokens_evac(0, 0, T_B0, None)
            split_hi(U_B + 4, N)
            act.wait_ge(t_ready, T_LFO + 1)
            A(lf_tok[:, 0:4, :], T[:, 0:64].rearrange("p (t c) -> p t c", t=4), ACT.Copy)
            A(lf_tok[0:NS, 4, :], T[0:NS, 64:80], ACT.Copy).then_inc(t_free, 1)
            act.wait_ge(t_free, T_LFO + 1)
            act.dma_start(o["b_lf_p"][0, 0].rearrange("(t p) h -> p t h", p=P), lf_tok[:, 0:4, :]).then_inc(out_sent, 16)
            act.dma_start(o["b_lf_s"][0, 0], lf_tok[0:NS, 4, :]).then_inc(out_sent, 16)
            act.wait_ge(cum_out, 16)
            act.wait_ge(out_sent, 16 * N_OUT_A)
            exp_unit(0, 32, 0, 8, pr_b, ps_b)
            g_evac(0, U_B + 3)
            v_tokens_evac(0, 0, T_B0 + 3)

            def b_body(it, last_turn):
                for r in range(2):
                    nxt = not (last_turn and r == 1)
                    for k in range(4):
                        n = 32 + 4 * r + k
                        u = U_B + 4 * (r + 1) + k
                        t = T_B + 13 * r + (0, 3, 5, 9)[k]
                        if not nxt:
                            t = T_B + 13 * r + (0 if k == 0 else 1 + 2 * k)
                        par2 = (r + 1) % 2
                        pair2 = 2 * it + r + 1
                        pT_evac(k, t, n, it, 8, 26, pT_b)
                        if not (last_turn and r == 1 and k == 3):
                            exp_unit((k + 1) % 4, n + 1, it, 8, pr_b, ps_b)
                        if nxt:
                            split_hi(u + 1, N, it, 8)
                            if k == 0:
                                q_evac(par2, u, it, 8)
                            if k == 2:
                                k_tokens_evac(par2, pair2, T_B + 13 * r + 7, 64 * (2 * it + r + 1), it, 26)
                                v_evac_b(u, it, 8)
                            if k == 3:
                                v_tokens_evac(par2, pair2, T_B + 13 * r + 11, it, 26)
                                g_evac(par2, u, it, 8)

            with act.Fori(0, PAIRS // 2 - 1) as it:
                b_body(it, False)
            b_body(PAIRS // 2 - 1, True)

            split_o(2 * PAIRS, ACT_OB)
            act.wait_ge(kv_sent, 16 * 4 * PAIRS)
            out_stage(U_OB, N, N, 3)
            norm(3, ACT_N3)
            ffn_half(U_F1, 2 * HT, N)
            ffn_half(U_F1 + FFN_N, 3 * HT, 0, 4)
            norm(4, None)
            for j in range(1, 10, 2):
                w = P if j % 5 < 4 else NS
                act.wait_ge(y_ready, j + 1)
                A(y_tok[0:w, j, :], y_bank[j % 6][0:w, :], ACT.Copy).then_inc(y_free[1], 1)

        @block.gpsimd
        def _(pool):
            TT, TS, CP = nc.gpsimd.tensor_tensor, nc.gpsimd.tensor_scalar, nc.gpsimd.tensor_copy

            def split_lo(u, n, it=0, per=0):
                pool.wait_ge(whi_done, per * it + u + 1)
                TT(w_lo[:, u % 2, 0:n], w_raw[:, u % 2, 0:n], w_hi[:, u % 2, 0:n].bitcast(F32), ALU.subtract)\
                    .then_inc(wlo_done, 1)

            nc.gpsimd.memset(cs_w[:, :, :], 0.0).then_inc(cs_zero, 1)
            nc.gpsimd.memset(ones[:, :], 1.0).then_inc(ones_done, 1)
            nc.gpsimd.memset(eps[:, :], EPS).then_inc(ones_done, 1)

            def sum_start(nz):
                if nz >= 1:
                    pool.wait_ge(ss_done, nz)
                nc.gpsimd.memset(ssq[:, :], 0.0).then_inc(ssq_done, 1)

            def sum_square(nz, m, it=0, per=0):
                pool.wait_ge(sq_done, per * it + KT * nz + m + 1)
                pool.wait_ge(ssq_done, per * it + KT * nz + m + 1)
                TT(ssq[:, :], ssq[:, :], sq[:, m % 2, :], ALU.add).then_inc(ssq_done, 1)

            sum_start(0)
            for kt in range(KT - 1):
                sum_square(0, kt)
            steps = [0]

            def rope(u):
                r = rope_of(u)
                pool.wait_ge(lin_free[u % 2], free_count(u))
                if u == U_K:
                    pool.wait_ge(rope_done, 5)
                raw, par = rawb[:, r % 2, :], permb[:, r % 2, :]
                TT(par, par, tables[:, 1, :], ALU.mult).then_inc(rope_step, 1)
                TT(raw, raw, tables[:, 0, :], ALU.mult).then_inc(rope_step, 1)
                steps[0] += 2
                pool.wait_ge(rope_step, steps[0])
                if u < U_V:
                    dst = kR[:, :]
                    if u == U_K + 1:
                        pool.wait_ge(kdup_done, 1)
                        pool.wait_ge(t_ready, T_K0 + 2)
                else:
                    dst = qo[:, u - U_Q, :]
                TT(dst, raw, par, ALU.add).then_inc(rope_done, 1)

            N = KT * P
            split_lo(U_KIW, KT * 72)
            split_lo(U_QI, N)
            split_lo(U_QI + 1, N)
            split_lo(U_QI + 2, N)
            split_lo(U_QI + 3, N)
            split_lo(U_K, N)
            split_lo(U_K + 1, N)
            split_lo(U_V, N)
            rope(U_K)
            split_lo(U_V + 1, N)
            rope(U_K + 1)
            split_lo(U_Q, N)
            split_lo(U_Q + 1, N)
            for j in range(1, PAIRS):
                split_lo(U_Q + j + 1, N)
                rope(U_Q + j - 1)

            def stage_q(pair, it=0):
                if pair >= 1:
                    pool.wait_ge(s_done, 8 * it + 4 * (pair - 1) + 1)
                CP(qS_a[:, pair % 2:pair % 2 + 1, :], qo[:, ds(2 * it + pair, 1), :]).then_inc(q_staged, 1)

            def split_pair(r, it):
                pool.wait_ge(o_free, 2 * it + r + 1)
                pair = ds(2 * it + r, 1)
                CP(act_hi[:, pair, :], qo[:, pair, :]).then_inc(ohi_done, 1)
                pool.wait_ge(ohi_done, 2 * it + r + 1)
                TT(act_lo[:, pair, :], qo[:, pair, :], act_hi[:, pair, :].bitcast(F32), ALU.subtract).then_inc(olo_done, 1)

            pool.wait_ge(q_staged, 1)
            with pool.Fori(0, PAIRS // 2 - 1) as it:
                stage_q(1, it)
                stage_q(2, it)
                split_pair(0, it)
                split_pair(1, it)
            stage_q(1, PAIRS // 2 - 1)
            split_pair(0, PAIRS // 2 - 1)

            def out_stage(u0, n, n_next, nz=None):
                def tile(r, it, per, cols, more=True):
                    if more:
                        split_lo(u0 + r + 1, cols, it, per)
                    if nz is not None and r < KT - 1:
                        sum_square(nz, r, it, per)

                if nz is not None:
                    sum_start(nz)
                with pool.Fori(0, KT // 2 - 1) as it:
                    for r in range(2):
                        tile(r, it, 2, n)
                tile(KT - 2, 0, 0, n)
                tile(KT - 1, 0, 0, n_next, bool(n_next))

            def ffn_half(u0, n_next, nz=None):
                with pool.Fori(0, HT - 1) as it:
                    for g in range(2):
                        split_lo(u0 + g + 1, N, it, 2)
                split_lo(u0 + 2 * HT - 1, N)
                split_lo(u0 + 2 * HT, HT * P)
                out_stage(u0 + 2 * HT, HT * P, n_next, nz)

            pool.wait_ge(o_free, PAIRS)
            pool.wait_ge(out_sent, 16 * 6)
            out_stage(U_OA, N, N, 1)
            ffn_half(U_F0, N)
            ffn_half(U_F0 + FFN_N, KT * 16, 2)
            for c in range(5):
                split_lo(U_B + c, N)

            def b_body(it, last_turn):
                for r in range(2):
                    for k in range(4):
                        if not (last_turn and r == 1):
                            split_lo(U_B + 4 * (r + 1) + k + 1, N, it, 8)

            with pool.Fori(0, PAIRS // 2 - 1) as it:
                b_body(it, False)
            b_body(PAIRS // 2 - 1, True)
            pool.wait_ge(o_free, 2 * PAIRS)
            pool.wait_ge(kv_sent, 16 * 4 * PAIRS)
            out_stage(U_OB, N, N, 3)
            ffn_half(U_F1, N)
            ffn_half(U_F1 + FFN_N, 0, 4)

        @block.vector
        def _(dve):
            V = nc.vector
            muls = [0]

            def tick(c):
                V.memset(cell[:, c:c + 1], 0.0)

            dve.wait_ge(const_in, 16)
            V.tensor_copy(ident_b[:, :], ident)
            V.tensor_copy(tri_b[:, :], tri)
            dve.wait_ge(t_ready, 1)
            V.tensor_copy(vecs[:, :], T[:, 0:P]).then_inc(t_free, 1)
            dve.wait_ge(t_ready, 2)
            V.tensor_copy(gains[:, :], T[:, 0:40]).then_inc(t_free, 1)
            for t in range(5):
                w = P if t < 4 else NS
                for h in range(2):
                    dve.wait_ge(t_ready, T_X + 2 * t + h + 1)
                    V.tensor_copy(x[:, 4 * h:4 * h + 4, t * P:t * P + w],
                                  T[:, :].rearrange("p (j c) -> p j c", j=4)[:, :, 0:w]).then_inc(t_free, 1)
            for h in range(2):
                dve.wait_ge(t_ready, T_KC + h + 1)
                V.tensor_copy(kT4[:, 2 * h:2 * h + 2, NP_:NP_ + PAST],
                              T[:, :].rearrange("p (g c) -> p g c", g=2)).then_inc(t_free, 1)
            dve.wait_ge(t_ready, T_KIC + 1)
            V.tensor_copy(kiT[:, NP_:NP_ + PAST], T[:, 0:PAST]).then_inc(t_free, 1)

            def ada_mods(b, t):
                dve.wait_ge(t_ready, t + 1)
                V.tensor_tensor(mods[:, 16 * b:16 * b + 16, :].rearrange("p (j c) s -> p j c s", j=4),
                                T[:, :].rearrange("p (c j s) -> p j c s", c=4, j=4)[:, :, :, 0:2],
                                vecs[:, 16 * b:16 * b + 16].rearrange("p (j c a) -> p j c a", j=4, a=1)
                                .broadcast_to([P, 4, 4, 2]), ALU.add).then_inc(t_free, 1)

            def multiplier(nz, t):
                dve.wait_ge(t_free, t + 1)
                V.tensor_scalar(mulA[:, nz, :, :], mods[:, SCALE[nz]:SCALE[nz] + KT, :], 1.0, None, ALU.add)\
                    .then_inc(muls_step, 1)
                muls[0] += 1
                dve.wait_ge(muls_step, muls[0])
                V.tensor_tensor(mulA[:, nz, :, :], mulA[:, nz, :, :],
                                gains[:, GAIN[nz]:GAIN[nz] + KT].rearrange("p (k a) -> p k a", a=1)
                                .broadcast_to([P, KT, 2]), ALU.mult).then_inc(muls_step, 1)
                muls[0] += 1
                dve.wait_ge(muls_step, muls[0])

            def norm(nz, act_base, between=None):
                dve.wait_ge(root_done, nz + 1)
                V.reciprocal(rstd[:, :], root[:, 0:5]).then_inc(rstd_done, 1)
                if between is not None:
                    between()
                dve.wait_ge(rstd_spread, nz + 1)
                parts = ((0, NP_, 0, S[:, 1, :]), (NP_, TOK, 1, S[:, 0, 2 * P - NS:2 * P]))
                for kt in range(KT):
                    for c0, c1, st, r in parts:
                        last = V.scalar_tensor_tensor(fo[:, kt, c0:c1], x[:, kt, c0:c1], mulA[:, nz, kt, st:st + 1], r,
                                                      ALU.mult, ALU.mult)
                    last.then_inc(y_done, 1)
                if act_base is None:
                    return
                for kt in range(KT):
                    dve.wait_ge(acthi_done, act_base + kt + 1)
                    for c0, c1, st, _ in parts:
                        last = V.scalar_tensor_tensor(act_lo[:, kt, c0:c1], fo[:, kt, c0:c1],
                                                      mods[:, SHIFT[nz] + kt, st:st + 1],
                                                      act_hi[:, kt, c0:c1].bitcast(F32), ALU.add, ALU.subtract)
                    last.then_inc(act_ready, 1)

            norm(0, ACT_N0, lambda: (ada_mods(0, T_ADA0), multiplier(0, T_ADA0)))

            for r, u in enumerate((U_KIW, U_QI, U_QI + 1, U_QI + 2, U_QI + 3)):
                if u == U_KIW:
                    dve.wait_ge(const_in, 32)
                dve.wait_ge(lin_free[u % 2], free_count(u))
                rows = 64 if u == U_KIW else P
                raw, par = rawb[0:rows, r % 2, :], permb[0:rows, r % 2, :]
                V.tensor_tensor(par, par, tables[0:rows, 3, :], ALU.mult).then_inc(ropev_step, 1)
                V.tensor_tensor(raw, raw, tables[0:rows, 2, :], ALU.mult).then_inc(ropev_step, 1)
                dve.wait_ge(ropev_step, 2 * r + 2)
                if u == U_KIW:
                    V.tensor_tensor(kiT[0:64, 0:NP_], raw[:, 0:NP_], par[:, 0:NP_], ALU.add)
                    V.tensor_tensor(kiT[0:64, NP_ + PAST:NK], raw[:, NP_:TOK], par[:, NP_:TOK], ALU.add)\
                        .then_inc(rope_done, 1)
                else:
                    V.tensor_tensor(qiT[:, u - U_QI, :], raw, par, ALU.add).then_inc(rope_done, 1)

            for n in range(16):
                qt, j = 3 - n // 4, n % 4
                rows, tt, off, nk = (P, qt, OFF[qt], (qt + 1) * P) if qt else (NS, 4, SOFF, PAST + NS)
                dve.wait_ge(rel_done, n + 1)
                dst = sc[0:rows, off:off + nk]
                for e in range(2):
                    w = wi_t[0:rows, tt, 2 * j + e:2 * j + e + 1]
                    if j == 0 and e == 0:
                        V.tensor_scalar(dst, rel[0:rows, 0, 0:nk], w, None, ALU.mult).then_inc(sc_step, 1)
                    else:
                        dve.wait_ge(sc_step, 2 * n + e)
                        V.scalar_tensor_tensor(dst, rel[0:rows, e, 0:nk], w, dst, ALU.mult, ALU.add)\
                            .then_inc(sc_step, 1)
            dve.wait_ge(sc_step, 32)
            for qt in range(1, 4):
                last = V.memset(sc[0:64, OFF[qt] + (qt + 1) * P - 64:OFF[qt] + (qt + 1) * P], FILL)
            last.then_inc(sc_step, 1)
            dve.wait_ge(sc_step, 33)
            tiles = [(P, OFF[qt], (qt + 1) * P) for qt in (3, 2, 1)] + [(NS, SOFF, PAST + NS)]

            def top_round(use, base, it):
                m = len(use)
                for c, (rows, off, nk) in enumerate(use):
                    V.max(top8[0:rows, c, :], sc[0:rows, off:off + nk]).then_inc(top_step, 1)
                dve.wait_ge(top_step, 2 * m * it + base + m)
                tick(8)
                for c, (rows, off, nk) in enumerate(use):
                    V.match_replace(sc[0:rows, off:off + nk], top8[0:rows, c, :], sc[0:rows, off:off + nk], TAKEN)\
                        .then_inc(top_step, 1)
                dve.wait_ge(top_step, 2 * m * it + base + 2 * m)

            with dve.Fori(0, TOPK_S // 8) as it:
                top_round(tiles, 0, it)
            with dve.Fori(0, (TOPK_P - TOPK_S) // 8) as it:
                top_round(tiles[:3], 8 * (TOPK_S // 8), it)
            V.tensor_scalar(sc[:, P:SOFF], sc[:, P:SOFF], TAKEN, NEG, ALU.not_equal, ALU.mult)
            V.memset(sc[:, 0:P], 0.0).then_inc(mask_done, 1)
            V.tensor_scalar(sc[0:NS, SOFF:], sc[0:NS, SOFF:], TAKEN, NEG, ALU.not_equal, ALU.mult).then_inc(mask_done, 1)
            dve.wait_ge(mask_done, 2)
            V.memset(sc[0:64, 64:P], NEG)
            V.tensor_copy(sc[64:P, SOFF:], sc[0:64, SOFF:]).then_inc(mask_done, 1)
            dve.wait_ge(mask_done, 3)

            def max_unit(k, n, it, per, pr, ps, bias, bias_s, bank):
                dve.wait_ge(s_done, per * it + n + 1)
                tick(n % 8)
                nk, c0 = (k + 1) * P, 384 if k == 0 else 0

                def one(out, in0, in1, acc):
                    return V.tensor_tensor_reduce(out=out, in0=in0, in1=in1, scale=-QSCALE, scalar=3.4e38,
                                                  op0=ALU.add, op1=ALU.min, accum_out=acc)

                if k == 0:
                    for e in range(2):
                        r = slice(64 * e, 64 * e + 64)
                        one(ps[r, :], bank[r, e, 0:PAST + NS], bias_s(e, r), negmax[r, 0, 2:3])
                for e in range(2):
                    last = one(probs(pr, k, e), bank[:, e, c0:c0 + nk], bias(e, k, nk), negmax[:, k, e:e + 1])
                last.then_inc(max_done, 1)

            def norm_unit(k, n, it, per, pr, ps):
                dve.wait_ge(exp_done, per * it + n + 1)
                w = 3 if k == 0 else 2
                V.reciprocal(rinv[:, k, 0:w], rowsum[:, k, 0:w]).then_inc(rinv_done, 1)
                dve.wait_ge(rinv_done, per * it + n + 1)
                for e in range(2):
                    last = V.tensor_scalar(probs(pr, k, e), probs(pr, k, e), rinv[:, k, e:e + 1], None, ALU.mult)
                if k == 0:
                    last = V.tensor_scalar(ps[:, :], ps[:, :], rinv[:, 0, 2:3], None, ALU.mult)
                last.then_inc(norm_done, 1)

            def pT_evac(k, t, n, it, per, tper, pT, pTs):
                dve.wait_ge(t_ready, tper * it + t + 1)
                if n >= 1:
                    dve.wait_ge(pv_done, per * it + n)
                if k == 0:
                    V.tensor_copy(pTs[:, 0:2, :], T[:, 0:2 * P].rearrange("p (b c) -> p b c", b=2))
                    V.tensor_copy(pTs[0:NS, 2, :], T[0:NS, 2 * P:3 * P]).then_inc(t_free, 1)
                else:
                    V.tensor_copy(pT[:, 1, 0:(k + 1) * P], T[:, 0:(k + 1) * P]).then_inc(t_free, 1)

            def bias_a(e, k, nk):
                return sc[:, OFF[k]:OFF[k] + nk]

            def bias_as(e, r):
                return sc[r, SOFF:]

            def ta_evac(n, it):
                k = n % 4
                dve.wait_ge(t2_ready, 8 * it + n + 1)
                if n >= 1:
                    dve.wait_ge(pv_done, 8 * it + n)
                if k == 0:
                    V.tensor_copy(pTs_a[:, 0:2, :], T2[:, 0:2 * P].rearrange("p (b c) -> p b c", b=2))
                    V.tensor_copy(pTs_a[0:NS, 2, :], T2[0:NS, 2 * P:3 * P]).then_inc(t2_free, 1)
                else:
                    V.tensor_copy(pT_a[:, 1, 0:(k + 1) * P], T2[:, 0:(k + 1) * P]).then_inc(t2_free, 1)

            def stage_k(group, it=0):
                V.tensor_copy(kS_a[:, :], kT4[:, ds(it + group, 1), :].rearrange("p a c -> p (a c)")).then_inc(k_staged, 1)

            def stage_v(group, it=0):
                if group >= 1:
                    dve.wait_ge(pv_done, 8 * it + 8 * group)
                cols = ds((it + group) * HD, HD)
                V.tensor_copy(vS_a[:, 0:6, :], v4[:, 0:6, cols])
                V.tensor_copy(vS_a[0:NS, 6, :], v4[0:NS, 6, cols]).then_inc(v_staged, 1)

            def a_body(it, last_turn):
                for n in range(8):
                    k, r = n % 4, n // 4
                    t = T_A + n
                    pair = ds(2 * it + r, 1)
                    if not (last_turn and n == 7):
                        norm_unit((k + 1) % 4, n + 1, it, 8, pr_a, ps_a)
                    ta_evac(n, it)
                    if not (last_turn and n >= 6):
                        max_unit((k + 2) % 4, n + 2, it, 8, pr_a, ps_a, bias_a, bias_as, (S, S2)[n % 2])
                    if n == 5 and not last_turn:
                        stage_k(1, it)
                if not last_turn:
                    stage_v(1, it)
                dve.wait_ge(t_ready, 9 * it + T_A + 9)
                V.tensor_tensor(mods[:, ds(16 * it + 48, 16), :].rearrange("p (j c) s -> p j c s", j=4),
                                T[:, :].rearrange("p (c j s) -> p j c s", c=4, j=4)[:, :, :, 0:2],
                                vecs[:, ds(16 * it + 48, 16)].rearrange("p (j c a) -> p j c a", j=4, a=1)
                                .broadcast_to([P, 4, 4, 2]), ALU.add).then_inc(t_free, 1)

            ada_mods(1, T_ADA1)
            u = U_Q + PAIRS - 1
            raw, par = rawb[:, rope_of(u) % 2, :], permb[:, rope_of(u) % 2, :]
            dve.wait_ge(lin_free[u % 2], free_count(u))
            V.tensor_tensor(par, par, tables[:, 1, :], ALU.mult).then_inc(ropev_step, 1)
            V.tensor_tensor(raw, raw, tables[:, 0, :], ALU.mult).then_inc(ropev_step, 1)
            dve.wait_ge(ropev_step, 12)
            dve.wait_ge(rope_done, rope_of(u))
            V.tensor_tensor(qo[:, PAIRS - 1, :], raw, par, ALU.add).then_inc(rope_done, 1)
            dve.wait_ge(rope_done, rope_of(u) + 1)
            dve.wait_ge(kdup_done, 2)
            dve.wait_ge(t_ready, T_V0 + 4)
            V.tensor_copy(qS_a[:, 0, :], qo[:, 0, :]).then_inc(q_staged, 1)
            stage_k(0)
            stage_v(0)
            max_unit(0, 0, 0, 8, pr_a, ps_a, bias_a, bias_as, S)
            max_unit(1, 1, 0, 8, pr_a, ps_a, bias_a, bias_as, S2)
            norm_unit(0, 0, 0, 8, pr_a, ps_a)
            ada_mods(2, T_ADA2)
            multiplier(1, T_ADA2)
            with dve.Fori(0, PAIRS // 2 - 1) as it:
                a_body(it, False)
            a_body(PAIRS // 2 - 1, True)
            dve.wait_ge(ohi_done, PAIRS)
            dve.wait_ge(olo_done, PAIRS - 1)
            V.tensor_tensor(act_lo[:, PAIRS - 1, :], qo[:, PAIRS - 1, :], act_hi[:, PAIRS - 1, :].bitcast(F32),
                            ALU.subtract).then_inc(olo_done, 1)

            def split_o(base):
                for kt in range(KT):
                    dve.wait_ge(acthi_done, base + kt + 1)
                    V.tensor_tensor(act_lo[:, kt, :], qo[:, kt, :], act_hi[:, kt, :].bitcast(F32), ALU.subtract)\
                        .then_inc(act_ready, 1)

            def residual(u0, gate):
                with dve.Fori(0, KT // 2) as it:
                    for r in range(2):
                        u = u0 + r
                        m = 2 * it + r
                        dve.wait_ge(mm_done, 2 * it + u + 1)
                        for h, c0, c1, st in ((0, 0, HALF, 0), (1, HALF, NP_, 0), (1, NP_, TOK, 1)):
                            dst = x[:, ds(m, 1), c0:c1].rearrange("p a c -> p (a c)")
                            last = V.scalar_tensor_tensor(dst, lin[:, u % 2, h, c0 - h * HALF:c1 - h * HALF],
                                                          mods[:, ds(m + gate, 1), st:st + 1].rearrange("p a c -> p (a c)"),
                                                          dst, ALU.mult, ALU.add)
                        last.then_inc(lin_free[u % 2], 1)

            def ffn_half(u0, hid_base, gate):
                with dve.Fori(0, HT) as it:
                    dve.wait_ge(mm_done, 2 * it + u0 + 2)
                    dve.wait_ge(lin_free[u0 % 2], it + free_count(u0))
                    V.tensor_tensor(hf[:, :].rearrange("p (h t) -> p h t", h=2), sg[:, :].rearrange("p (h t) -> p h t", h=2),
                                    lin[:, (u0 + 1) % 2, :, 0:HALF], ALU.mult).then_inc(lin_free[(u0 + 1) % 2], 1)
                    dve.wait_ge(hidhi_done, it + hid_base + 1)
                    V.tensor_tensor(hid_lo[:, ds(it, 1), :].rearrange("p a c -> p (a c)"), hf[:, :],
                                    hid_hi[:, ds(it, 1), :].rearrange("p a c -> p (a c)").bitcast(F32), ALU.subtract)\
                        .then_inc(hid_ready, 1)
                residual(u0 + 2 * HT, gate)

            residual(U_OA, 16)
            norm(1, ACT_N1)
            ffn_half(U_F0, 0, 40)
            ffn_half(U_F0 + FFN_N, HT, 40)
            for nz, bt in ((2, 3), (3, 5), (4, 6)):
                multiplier(nz, T_ADA[bt])
            norm(2, ACT_N2)

            steps = [0]

            def chain(ins):
                ins.then_inc(lf_dve, 1)
                steps[0] += 1
                dve.wait_ge(lf_dve, steps[0])

            dve.wait_ge(lf_act, 2)
            chain(V.tensor_scalar(ub[:, :], eb[:, :], 1.0, None, ALU.add))
            chain(V.memset(one_row[:, :], 1.0))
            dve.wait_ge(lf_act, 3)
            chain(V.tensor_scalar(ub[:, :], ub[:, :], -1.0, None, ALU.add))
            chain(V.tensor_tensor(lb[:, :], lb[:, :], eb[:, :], ALU.mult))
            chain(V.scalar_tensor_tensor(lb[:, :], ub[:, :], 0.0, lb[:, :], ALU.is_equal, ALU.add))
            chain(V.scalar_tensor_tensor(ub[:, :], ub[:, :], 0.0, ub[:, :], ALU.is_equal, ALU.add))
            chain(V.reciprocal(ub[:, :], ub[:, :]))
            chain(V.tensor_tensor(lb[:, :], lb[:, :], ub[:, :], ALU.mult))
            chain(V.scalar_tensor_tensor(ub[:, :], lb[:, :], 1.0, eb[:, :], ALU.is_equal, ALU.mult))
            chain(V.scalar_tensor_tensor(eb[:, :], lb[:, :], 1.0, lb[:, :], ALU.not_equal, ALU.mult))
            chain(V.tensor_tensor(eb[:, :], eb[:, :], ub[:, :], ALU.add))
            chain(V.scalar_tensor_tensor(lb[:, :], zb[:, :], 0.0, eb[:, :], ALU.min, ALU.subtract))
            assert steps[0] == LF_DONE
            dve.wait_ge(t_ready, T_LF + 1)
            V.tensor_copy(lfs[:, 0:PAST], T[0:16, 0:PAST]).then_inc(t_free, 1)
            chain(V.tensor_copy(lfs[:, PAST:], lb[:, NP_:TOK]))
            dve.wait_ge(t_free, T_LF + 1)
            chain(V.tensor_tensor_scan(cum[:, 0:NP_], one_row[:, 0:NP_], lb[:, 0:NP_], 0.0, ALU.mult, ALU.add))
            chain(V.tensor_tensor_scan(cum[:, NP_:], one_row[:, 0:PAST + NS], lfs[:, :], 0.0, ALU.mult, ALU.add))
            chain(V.tensor_scalar(cum[:, :], cum[:, :], -1.0 / QSCALE, None, ALU.mult))
            assert steps[0] == LF_CUM

            def k_evac(par, u, it=0, per=0):
                dve.wait_ge(mm_done, per * it + u + 1)
                V.tensor_copy(kS_b[:, par, 0:HALF], lin[:, u % 2, 0, 0:HALF])
                V.tensor_copy(kS_b[:, par, HALF:NP_], lin[:, u % 2, 1, 0:NP_ - HALF])
                V.tensor_copy(kS_b[:, par, NP_ + PAST:NK], lin[:, u % 2, 1, NP_ - HALF:HALF])\
                    .then_inc(lin_free[u % 2], 1)

            def gate(par, u, it=0, per=0):
                dve.wait_ge(lin_free[u % 2], (per // 2) * it + free_count(u))
                V.tensor_scalar(gsig[:, par, :], gsig[:, par, :], 1.0, None, ALU.add).then_inc(gsig_step, 1)

            def gate_piece(r, piece, it):
                if piece == 0:
                    dve.wait_ge(gsig_step, 12 * it + 6 * r + 1)
                cols = slice(NP_, TOK) if piece == 0 else slice((piece - 1) * P, piece * P)
                V.reciprocal(gsig[:, r, cols], gsig[:, r, cols]).then_inc(gsig_step, 1)

            def bias_b(par):
                return lambda e, k, nk: bk[:, par, e, 0:nk]

            def bias_bs(par):
                return lambda e, r: bk[r, par, e, NP_:NK]

            def b_body(it, last_turn):
                for r in range(2):
                    nxt = not (last_turn and r == 1)
                    for k in range(4):
                        n = 32 + 4 * r + k
                        u = U_B + 4 * (r + 1) + k
                        t = T_B + 13 * r + (0, 3, 5, 9)[k]
                        if not nxt:
                            t = T_B + 13 * r + (0 if k == 0 else 1 + 2 * k)
                        par2 = (r + 1) % 2
                        if not (last_turn and r == 1 and k == 3):
                            p2 = (r + (k == 3)) % 2
                            max_unit((k + 1) % 4, n + 1, it, 8, pr_b, ps_b, bias_b(p2), bias_bs(p2), S)
                        pT_evac(k, t + 1, n, it, 8, 26, pT_b, pTs_b)
                        if not (last_turn and r == 1 and k == 3):
                            norm_unit((k + 1) % 4, n + 1, it, 8, pr_b, ps_b)
                        pair = 2 * it + r
                        if k == 0:
                            gate_piece(r, 0, it)
                            dve.wait_ge(gsig_step, 12 * it + 6 * r + 2)
                            dve.wait_ge(t_ready, 26 * it + t + 3)
                            V.tensor_tensor(qo[:, ds(pair, 1), NP_:TOK].rearrange("p a c -> p (a c)"), T[:, 0:NS],
                                            gsig[:, r, NP_:TOK], ALU.mult).then_inc(t_free, 1)
                        gate_piece(r, k + 1, it)
                        if k == 3:
                            dve.wait_ge(gsig_step, 12 * it + 6 * r + 6)
                            dve.wait_ge(pv_done, 8 * it + n + 1)
                            V.tensor_tensor(qo[:, ds(pair, 1), 0:NP_].rearrange("p a c -> p (a c)"), O[:, :],
                                            gsig[:, r, 0:NP_], ALU.mult).then_inc(o_free, 1)
                        if nxt and k == 1:
                            k_evac(par2, u, it, 8)
                        if nxt and k == 3:
                            gate(par2, u, it, 8)

            dve.wait_ge(bk_in[0], 32)
            dve.wait_ge(out_sent, 16 * N_OUT_A)
            max_unit(0, 32, 0, 8, pr_b, ps_b, bias_b(0), bias_bs(0), S)
            norm_unit(0, 32, 0, 8, pr_b, ps_b)
            gate(0, U_B + 3)
            with dve.Fori(0, PAIRS // 2 - 1) as it:
                b_body(it, False)
            b_body(PAIRS // 2 - 1, True)

            split_o(ACT_OB)
            residual(U_OB, 64)
            norm(3, ACT_N3)
            ffn_half(U_F1, 2 * HT, 88)
            ffn_half(U_F1 + FFN_N, 3 * HT, 88)
            norm(4, None)
            for j in range(0, 10, 2):
                w = P if j % 5 < 4 else NS
                dve.wait_ge(y_ready, j + 1)
                V.tensor_copy(y_tok[0:w, j, :], y_bank[j % 6][0:w, :]).then_inc(y_free[0], 1)


T_ADA = [T_ADA0, T_ADA1, T_ADA2] + [T_A + 9 * j + 8 for j in range(4)]
SHIFT = [0, 24, 48, 72, 96]
SCALE = [8, 32, 56, 80, 104]
GAIN = [0, 16, 8, 24, 32]
N_OUT_A = 8
LF_DONE, LF_CUM = 12, 16
KVC_ROUND = {U_B + 1: 1, U_B + 5: 1, U_B + 9: 2}

_INS = ["x_prompt", "x_sample", "cache_a_k", "cache_a_v", "cache_a_kidx", "cache_b_k", "cache_b_v", "cache_b_logf",
        "c_prompt", "c_sample", "w_ada", "b_ada", "g_mix", "g_ffn", "w_in_a", "w_out_a", "w_in_b", "b_forget",
        "w_out_b", "w_ffn_in", "w_ffn_out", "w_ada_final", "b_ada_final", "g_final"]
_OUTS = [("y_p", (1, 512, 1024)), ("y_s", (1, 64, 1024)),
         ("a_k_p", (1, 1, 512, 4, 64)), ("a_v_p", (1, 1, 512, 4, 64)), ("kidx_p", (1, 1, 512, 64)),
         ("b_k_p", (1, 1, 512, 16, 64)), ("b_v_p", (1, 1, 512, 16, 64)), ("b_lf_p", (1, 1, 512, 16)),
         ("a_k_s", (1, 1, 64, 4, 64)), ("a_v_s", (1, 1, 64, 4, 64)), ("kidx_s", (1, 1, 64, 64)),
         ("b_k_s", (1, 1, 64, 16, 64)), ("b_v_s", (1, 1, 64, 16, 64)), ("b_lf_s", (1, 1, 64, 16))]


def kernel(**inputs):
    import concourse.bacc as _bacc
    from concourse.bass_utils import run_bass_kernel_spmd as _run

    nc = _bacc.Bacc("TRN2", target_bir_lowering=False, num_devices=1)
    arrays, ins, outs = {}, {}, {}
    for name in _INS:
        arr = np.ascontiguousarray(inputs[name])
        arrays[f"in_{name}"] = arr
        ins[name] = nc.dram_tensor(f"in_{name}", arr.shape, mybir.dt.from_np(arr.dtype), kind="ExternalInput").ap()
    consts = host_constants()
    arrays["in_consts"] = consts
    ins["consts"] = nc.dram_tensor("in_consts", consts.shape, F32, kind="ExternalInput").ap()
    for name, shape in _OUTS:
        outs[name] = nc.dram_tensor(f"out_{name}", shape, F32, kind="ExternalOutput").ap()
    encoder_step(nc, ins, outs)
    r = _run(nc, [arrays], core_ids=[0])
    return tuple(r.results[0][f"out_{name}"] for name, _ in _OUTS)
```
